# Optimizing a Trainium2 kernel written in Bass

```python
import math
import jax, jax.numpy as jnp
from jax import lax
import numpy as np

D_MODEL = 1024
BATCH = 1
SEQ = 512
DEPTH = 2

N_A_LAYERS = DEPTH // 2
N_B_LAYERS = DEPTH - N_A_LAYERS

DN_HEADS = 8
DN_HEAD_DIM = D_MODEL // DN_HEADS
DN_WIDTH = DN_HEADS * DN_HEAD_DIM
CONV_K = 4
DN_CHUNK = 64

DA_HEADS = 8
DA_HEAD_DIM = D_MODEL // (2 * DA_HEADS)
DA_V_DIM = 2 * DA_HEAD_DIM
DA_QK_WIDTH = 2 * DA_HEADS * DA_HEAD_DIM
DA_WIDTH = DA_HEADS * DA_V_DIM
Q_BLOCK = 128

N_GROUPS = 4
EXPERTS_PER_GROUP = 8
N_EXPERTS = N_GROUPS * EXPERTS_PER_GROUP
TOP_K = 2
EXPERT_FF = D_MODEL // 2
MOE_BLOCK = 128

ALPHA = (2 * DEPTH) ** 0.25
BETA_INIT = (8 * DEPTH) ** -0.25
LN_EPS = 1e-5
RMS_EPS = 1e-6


def layer_norm(x, g, b):
    xf = x.astype(jnp.float32)
    mu = jnp.mean(xf, axis=-1, keepdims=True)
    var = jnp.mean(jnp.square(xf - mu), axis=-1, keepdims=True)
    return ((xf - mu) * lax.rsqrt(var + LN_EPS) * g + b).astype(x.dtype)

def rms_norm(x, w):
    xf = x.astype(jnp.float32)
    return xf * lax.rsqrt(jnp.mean(jnp.square(xf), axis=-1, keepdims=True) + RMS_EPS) * w.astype(jnp.float32)

def l2_normalize(x):
    xf = x.astype(jnp.float32)
    return xf * lax.rsqrt(jnp.sum(jnp.square(xf), axis=-1, keepdims=True) + RMS_EPS)

def causal_depthwise_conv(x, w):
    k_width, t = w.shape[0], x.shape[1]
    xp = jnp.pad(x, ((0, 0), (k_width - 1, 0), (0, 0)))
    y = xp[:, 0:t] * w[0]
    for j in range(1, k_width):
        y = y + xp[:, j:j + t] * w[j]
    return y

def chunked_gated_delta_rule(q, k, v, g, beta):
    b, t, h, dk = q.shape
    dv = v.shape[-1]
    n, c = t // DN_CHUNK, DN_CHUNK

    def to_chunks(a):
        return jnp.moveaxis(a.reshape((b, n, c, h) + a.shape[3:]), 3, 1)

    q = to_chunks(q * dk ** -0.5)
    k = to_chunks(k)
    v = to_chunks(v.astype(jnp.float32))
    gc = jnp.cumsum(to_chunks(g), axis=-1)
    beta = to_chunks(beta)
    idx = jnp.arange(c)
    causal = idx[:, None] >= idx[None, :]
    strict = idx[:, None] > idx[None, :]
    decay = jnp.exp(jnp.where(causal, gc[..., :, None] - gc[..., None, :], -jnp.inf))
    k_beta = k * beta[..., None]
    a_mat = jnp.where(strict, jnp.einsum('bhnid,bhnjd->bhnij', k_beta, k) * decay, 0.0)
    rhs = jnp.concatenate([v * beta[..., None], k_beta * jnp.exp(gc)[..., None]], axis=-1)
    sol = lax.linalg.triangular_solve(a_mat + jnp.eye(c, dtype=jnp.float32), rhs,
                                      left_side=True, lower=True, unit_diagonal=True)
    u, w = sol[..., :dv], sol[..., dv:]
    attn = jnp.where(causal, jnp.einsum('bhnid,bhnjd->bhnij', q, k) * decay, 0.0)
    q_dec = q * jnp.exp(gc)[..., None]
    k_dec = k * jnp.exp(gc[..., -1:] - gc)[..., None]
    g_last = jnp.exp(gc[..., -1])

    def step(state, xs):
        u_i, w_i, q_i, k_i, attn_i, gl_i = xs
        v_new = u_i - jnp.einsum('bhcd,bhdv->bhcv', w_i, state)
        o_i = jnp.einsum('bhcd,bhdv->bhcv', q_i, state) + jnp.einsum('bhij,bhjv->bhiv', attn_i, v_new)
        state = state * gl_i[..., None, None] + jnp.einsum('bhcd,bhcv->bhdv', k_i, v_new)
        return state, o_i

    xs = tuple(jnp.moveaxis(a, 2, 0) for a in (u, w, q_dec, k_dec, attn, g_last))
    state0 = jnp.zeros((b, h, dk, dv), jnp.float32)
    _, o = lax.scan(step, state0, xs)
    return o.transpose(1, 0, 3, 2, 4).reshape(b, t, h, dv)

def gated_deltanet(x, w_in, conv_w, a_log, dt_bias, norm_w, w_out):
    b, t, _ = x.shape
    proj = x @ w_in
    qkv = jax.nn.silu(causal_depthwise_conv(proj[..., :3 * DN_WIDTH], conv_w))
    qkv = qkv.reshape(b, t, 3, DN_HEADS, DN_HEAD_DIM)
    q = l2_normalize(qkv[:, :, 0])
    k = l2_normalize(qkv[:, :, 1])
    v = qkv[:, :, 2]
    z = proj[..., 3 * DN_WIDTH:4 * DN_WIDTH].reshape(b, t, DN_HEADS, DN_HEAD_DIM)
    beta = jax.nn.sigmoid(proj[..., 4 * DN_WIDTH:4 * DN_WIDTH + DN_HEADS].astype(jnp.float32))
    alpha_logit = proj[..., 4 * DN_WIDTH + DN_HEADS:].astype(jnp.float32)
    g = -jnp.exp(a_log.astype(jnp.float32)) * jax.nn.softplus(alpha_logit + dt_bias.astype(jnp.float32))
    o = chunked_gated_delta_rule(q, k, v, g, beta)
    o = rms_norm(o, norm_w) * jax.nn.silu(z.astype(jnp.float32))
    return o.reshape(b, t, DN_WIDTH).astype(x.dtype) @ w_out

def shared_kv(x, kv_w):
    b, t, _ = x.shape
    kv = x @ kv_w
    keys = kv[..., :DA_QK_WIDTH].reshape(b, t, DA_HEADS, 2, DA_HEAD_DIM).transpose(3, 0, 2, 1, 4)
    vals = kv[..., DA_QK_WIDTH:].reshape(b, t, DA_HEADS, DA_V_DIM).transpose(0, 2, 1, 3)
    return keys, vals

def differential_attention(x, keys, vals, w_q, lam_p, subln_w, w_out, lam_init):
    b, t, _ = x.shape
    nb = t // Q_BLOCK
    q = (x @ w_q).reshape(b, nb, Q_BLOCK, DA_HEADS, 2, DA_HEAD_DIM).transpose(1, 4, 0, 3, 2, 5)
    lp = lam_p.astype(jnp.float32)
    lam = jnp.exp(jnp.sum(lp[0] * lp[1])) - jnp.exp(jnp.sum(lp[2] * lp[3])) + lam_init
    key_pos = jnp.arange(t)
    scale = DA_HEAD_DIM ** -0.5

    def block(args):
        q_blk, blk = args
        query_pos = blk * Q_BLOCK + jnp.arange(Q_BLOCK)
        mask = key_pos[None, :] <= query_pos[:, None]
        s = jnp.einsum('sbhqd,sbhkd->sbhqk', q_blk, keys).astype(jnp.float32) * scale
        p = jax.nn.softmax(jnp.where(mask, s, -jnp.inf), axis=-1)
        a = p[0] - lam * p[1]
        return jnp.einsum('bhqk,bhkv->bhqv', a.astype(vals.dtype), vals)

    o = lax.map(block, (q, jnp.arange(nb)))
    o = o.transpose(1, 0, 3, 2, 4).reshape(b, t, DA_HEADS, DA_V_DIM)
    o = rms_norm(o, subln_w) * (1.0 - lam_init)
    return o.reshape(b, t, DA_WIDTH).astype(x.dtype) @ w_out

def hierarchical_moe(x, w_group, w_expert, w13, w2):
    b, t, d = x.shape
    n = b * t
    m = n * TOP_K
    xf = x.reshape(n, d)
    group_prob = jax.nn.softmax((xf @ w_group).astype(jnp.float32), axis=-1)
    p_group, group_idx = lax.top_k(group_prob, 1)
    expert_logits = (xf @ w_expert).astype(jnp.float32).reshape(n, N_GROUPS, EXPERTS_PER_GROUP)
    in_group = expert_logits[jnp.arange(n), group_idx[:, 0]]
    top_p, top_i = lax.top_k(jax.nn.softmax(in_group, axis=-1), TOP_K)
    gate = (p_group * top_p / jnp.sum(top_p, axis=-1, keepdims=True)).reshape(m)
    expert_id = (group_idx * EXPERTS_PER_GROUP + top_i).reshape(m)
    token_id = jnp.repeat(jnp.arange(n), TOP_K)
    order = jnp.argsort(expert_id)
    eid_s, tok_s, gate_s = expert_id[order], token_id[order], gate[order]
    counts = jnp.bincount(expert_id, length=N_EXPERTS)
    start = jnp.cumsum(counts) - counts
    padded = (counts + MOE_BLOCK - 1) // MOE_BLOCK * MOE_BLOCK
    pad_end = jnp.cumsum(padded)
    pad_start = pad_end - padded
    dest = pad_start[eid_s] + jnp.arange(m) - start[eid_s]
    n_rows = (m + N_EXPERTS * (MOE_BLOCK - 1) + MOE_BLOCK - 1) // MOE_BLOCK * MOE_BLOCK
    n_blocks = n_rows // MOE_BLOCK
    row_tok = jnp.zeros((n_rows,), jnp.int32).at[dest].set(tok_s)
    row_gate = jnp.zeros((n_rows,), x.dtype).at[dest].set(gate_s.astype(x.dtype))
    block_eid = jnp.minimum(jnp.searchsorted(pad_end, jnp.arange(n_blocks) * MOE_BLOCK, side='right'),
                            N_EXPERTS - 1)
    x_rows = xf[row_tok].reshape(n_blocks, MOE_BLOCK, d)

    def expert_block(args):
        xb, e = args
        hcat = xb @ w13[e]
        hid = jax.nn.silu(hcat[:, :EXPERT_FF]) * hcat[:, EXPERT_FF:]
        return hid @ w2[e]

    y_rows = lax.map(expert_block, (x_rows, block_eid)).reshape(n_rows, d)
    y = jax.ops.segment_sum(y_rows * row_gate[:, None], row_tok, num_segments=n)
    return y.reshape(b, t, d)

def lambda_init(layer_idx):
    return 0.8 - 0.6 * math.exp(-0.3 * layer_idx)

def first_inputs(seed: int = 0) -> dict:
    key = jax.random.key(seed)
    ks = jax.random.split(key, 24)
    f32 = jnp.float32
    D = D_MODEL

    def nrm(k, shape, scale):
        return jax.random.normal(k, shape, f32) * scale

    in_a = 4 * DN_WIDTH + 2 * DN_HEADS
    x = nrm(ks[0], (BATCH, SEQ, D), 1.0)
    a_w_in = nrm(ks[1], (N_A_LAYERS, D, in_a), D ** -0.5)
    a_conv_w = nrm(ks[2], (N_A_LAYERS, CONV_K, 3 * DN_WIDTH), CONV_K ** -0.5)
    a_a_log = jnp.log(jax.random.uniform(ks[3], (N_A_LAYERS, DN_HEADS), f32, 1.0, 16.0))
    dt = jnp.exp(jax.random.uniform(ks[4], (N_A_LAYERS, DN_HEADS), f32, math.log(1e-3), math.log(1e-1)))
    a_dt_bias = dt + jnp.log(-jnp.expm1(-dt))
    a_norm_w = 1.0 + nrm(ks[5], (N_A_LAYERS, DN_HEAD_DIM), 0.02)
    a_w_out = nrm(ks[6], (N_A_LAYERS, DN_WIDTH, D), DN_WIDTH ** -0.5 * BETA_INIT)
    kv_w = nrm(ks[7], (D, DA_QK_WIDTH + DA_WIDTH), D ** -0.5)
    b_w_q = nrm(ks[8], (N_B_LAYERS, D, DA_QK_WIDTH), D ** -0.5)
    b_lambda = nrm(ks[9], (N_B_LAYERS, 4, DA_HEAD_DIM), 0.1)
    b_subln_w = 1.0 + nrm(ks[10], (N_B_LAYERS, DA_V_DIM), 0.02)
    b_w_out = nrm(ks[11], (N_B_LAYERS, DA_WIDTH, D), DA_WIDTH ** -0.5 * BETA_INIT)
    ln_mix_g = 1.0 + nrm(ks[12], (DEPTH, D), 0.02)
    ln_mix_b = nrm(ks[13], (DEPTH, D), 0.02)
    ln_ffn_g = 1.0 + nrm(ks[14], (DEPTH, D), 0.02)
    ln_ffn_b = nrm(ks[15], (DEPTH, D), 0.02)
    moe_w_group = nrm(ks[16], (DEPTH, D, N_GROUPS), D ** -0.5)
    moe_w_expert = nrm(ks[17], (DEPTH, D, N_EXPERTS), D ** -0.5)
    moe_w13 = nrm(ks[18], (DEPTH, N_EXPERTS, D, 2 * EXPERT_FF), D ** -0.5)
    moe_w2 = nrm(ks[19], (DEPTH, N_EXPERTS, EXPERT_FF, D), EXPERT_FF ** -0.5 * BETA_INIT)
    return {'x': x, 'a_w_in': a_w_in, 'a_conv_w': a_conv_w, 'a_a_log': a_a_log, 'a_dt_bias': a_dt_bias,
            'a_norm_w': a_norm_w, 'a_w_out': a_w_out, 'kv_w': kv_w, 'b_w_q': b_w_q, 'b_lambda': b_lambda,
            'b_subln_w': b_subln_w, 'b_w_out': b_w_out, 'ln_mix_g': ln_mix_g, 'ln_mix_b': ln_mix_b,
            'ln_ffn_g': ln_ffn_g, 'ln_ffn_b': ln_ffn_b, 'moe_w_group': moe_w_group,
            'moe_w_expert': moe_w_expert, 'moe_w13': moe_w13, 'moe_w2': moe_w2}

def first_block(x, a_w_in, a_conv_w, a_a_log, a_dt_bias, a_norm_w, a_w_out, kv_w, b_w_q, b_lambda,
              b_subln_w, b_w_out, ln_mix_g, ln_mix_b, ln_ffn_g, ln_ffn_b, moe_w_group, moe_w_expert,
              moe_w13, moe_w2):
    h = x
    keys, vals = None, None
    for layer in range(DEPTH):
        if layer < N_A_LAYERS:
            mix = gated_deltanet(h, a_w_in[layer], a_conv_w[layer], a_a_log[layer], a_dt_bias[layer],
                                 a_norm_w[layer], a_w_out[layer])
        else:
            j = layer - N_A_LAYERS
            if j == 0:
                keys, vals = shared_kv(h, kv_w)
            mix = differential_attention(h, keys, vals, b_w_q[j], b_lambda[j], b_subln_w[j], b_w_out[j],
                                         lambda_init(layer))
        h = layer_norm(ALPHA * h + mix, ln_mix_g[layer], ln_mix_b[layer])
        ffn = hierarchical_moe(h, moe_w_group[layer], moe_w_expert[layer], moe_w13[layer], moe_w2[layer])
        h = layer_norm(ALPHA * h + ffn, ln_ffn_g[layer], ln_ffn_b[layer])
    return h


GRID_W = 64
CTX_LEN = 256
HEAD_DIM = 64
NA_HEADS = 8
NA_WIDTH = NA_HEADS * HEAD_DIM
WIN_R = 8
WIN_C = 16
GQA_Q_HEADS = 8
GQA_KV_HEADS = 2
GQA_GROUP = GQA_Q_HEADS // GQA_KV_HEADS
GQA_WIDTH = GQA_Q_HEADS * HEAD_DIM
GQA_KV_WIDTH = GQA_KV_HEADS * HEAD_DIM
ROPE_THETA = 10000.0
ROT_AXIS = HEAD_DIM // 2
EPS = 1e-6
SPLIT_SIZES = (NA_WIDTH, NA_WIDTH, GQA_KV_WIDTH, GQA_KV_WIDTH,
               NA_WIDTH, GQA_WIDTH, NA_WIDTH, GQA_WIDTH, D_MODEL, D_MODEL)
KV_COLS = 2 * NA_WIDTH + 2 * GQA_KV_WIDTH
IN_COLS = sum(SPLIT_SIZES)


def _split(p, sizes):
    outs, off = [], 0
    for s in sizes:
        outs.append(p[..., off:off + s])
        off += s
    return outs

def _rmsnorm(x, g):
    xf = x.astype(jnp.float32)
    y = xf * lax.rsqrt(jnp.mean(xf * xf, axis=-1, keepdims=True) + EPS)
    return (y * g.astype(jnp.float32)).astype(x.dtype)

def _rope_axis(x, pos):
    half = ROT_AXIS // 2
    inv = 1.0 / (ROPE_THETA ** (jnp.arange(half, dtype=jnp.float32) / half))
    ang = pos.astype(jnp.float32)[:, None] * inv[None, :]
    cos = jnp.cos(ang)[None, :, None, :].astype(x.dtype)
    sin = jnp.sin(ang)[None, :, None, :].astype(x.dtype)
    x1, x2 = x[..., :half], x[..., half:]
    return jnp.concatenate([x1 * cos - x2 * sin, x2 * cos + x1 * sin], axis=-1)

def _rope_2d(x, pos_row, pos_col):
    return jnp.concatenate([_rope_axis(x[..., :ROT_AXIS], pos_row),
                            _rope_axis(x[..., ROT_AXIS:], pos_col)], axis=-1)

def _attend(q, k, v):
    s = jnp.einsum('bqkgd,btkd->bkgqt', q, k).astype(jnp.float32) * (HEAD_DIM ** -0.5)
    p = jax.nn.softmax(s, axis=-1).astype(v.dtype)
    return jnp.einsum('bkgqt,btkd->bqkgd', p, v)

def _na_latent(q, k, v, kc, vc, rpb, rows):
    B = q.shape[0]
    wr = min(WIN_R, rows)
    qg = q.reshape(B, rows, GRID_W, NA_HEADS, HEAD_DIM)
    kg = k.reshape(B, rows, GRID_W, NA_HEADS, HEAD_DIM)
    vg = v.reshape(B, rows, GRID_W, NA_HEADS, HEAD_DIM)
    cols = np.arange(GRID_W)
    cs = np.clip(cols - WIN_C // 2, 0, GRID_W - WIN_C)
    col_idx_np = (cs[:, None] + np.arange(WIN_C)[None, :]).astype(np.int32)
    col_off_np = (col_idx_np - cols[:, None] + (WIN_C - 1)).astype(np.int32)
    rws = np.arange(rows)
    rs = np.clip(rws - wr // 2, 0, rows - wr)
    row_idx_np = (rs[:, None] + np.arange(wr)[None, :]).astype(np.int32)
    row_off_np = (row_idx_np - rws[:, None] + (WIN_R - 1)).astype(np.int32)
    col_idx = jnp.asarray(col_idx_np)
    bias_all = rpb[:, row_off_np[:, :, None, None], col_off_np[None, None, :, :]]
    bias_all = jnp.transpose(bias_all, (1, 0, 3, 2, 4)).astype(jnp.float32)
    q_rows = jnp.transpose(qg, (1, 0, 2, 3, 4))
    scale = HEAD_DIM ** -0.5

    def row_block(args):
        qr, ridx, bias = args
        kb = jnp.take(kg, ridx, axis=1)
        vb = jnp.take(vg, ridx, axis=1)
        kw = jnp.take(kb, col_idx, axis=2)
        vw = jnp.take(vb, col_idx, axis=2)
        s_win = jnp.einsum('bchd,bicjhd->bhcij', qr, kw).astype(jnp.float32) * scale + bias[None]
        s_ctx = jnp.einsum('bchd,blhd->bhcl', qr, kc).astype(jnp.float32) * scale
        s = jnp.concatenate([s_win.reshape(B, NA_HEADS, GRID_W, wr * WIN_C), s_ctx], axis=-1)
        p = jax.nn.softmax(s, axis=-1).astype(v.dtype)
        p_win = p[..., :wr * WIN_C].reshape(B, NA_HEADS, GRID_W, wr, WIN_C)
        p_ctx = p[..., wr * WIN_C:]
        return (jnp.einsum('bhcij,bicjhd->bchd', p_win, vw)
                + jnp.einsum('bhcl,blhd->bchd', p_ctx, vc))

    out = lax.map(row_block, (q_rows, jnp.asarray(row_idx_np), bias_all))
    return jnp.transpose(out, (1, 0, 2, 3, 4)).reshape(B, rows * GRID_W, NA_WIDTH)

def _gqa_latent(q, k_all, v_all):
    B, S = q.shape[0], q.shape[1]
    nb = S // Q_BLOCK
    qb = q.reshape(B, nb, Q_BLOCK, GQA_KV_HEADS, GQA_GROUP, HEAD_DIM)
    qb = jnp.transpose(qb, (1, 0, 2, 3, 4, 5))
    out = lax.map(lambda qq: _attend(qq, k_all, v_all), qb)
    return jnp.transpose(out, (1, 0, 2, 3, 4, 5)).reshape(B, S, GQA_WIDTH)

def _merge(a_att, b_att, a_z, b_z, g_a, g_b, w_o_a, w_o_b, w_out):
    o_a = (a_att * jax.nn.silu(a_z)) @ w_o_a
    o_b = (b_att * jax.nn.silu(b_z)) @ w_o_b
    merged = jax.nn.sigmoid(g_a) * o_a + jax.nn.sigmoid(g_b) * o_b
    return merged @ w_out

def _layer(x, ctx, c, c_ctx, w_ada, b_ada, norm_g, w_in, q_norm_a, k_norm_a,
           q_norm_b, k_norm_b, rpb, w_o_a, w_o_b, w_out, pos_row, pos_col, update_ctx):
    B, S, _ = x.shape
    L = ctx.shape[1]
    rows = S // GRID_W
    mod_x = jax.nn.silu(c) @ w_ada + b_ada
    shift_x, scale_x, gate_x = jnp.split(mod_x[:, None, :], 3, axis=-1)
    mod_c = jax.nn.silu(c_ctx) @ w_ada + b_ada
    shift_c, scale_c, gate_c = jnp.split(mod_c, 3)
    hx = _rmsnorm(x, norm_g) * (1.0 + scale_x) + shift_x
    hc = _rmsnorm(ctx, norm_g) * (1.0 + scale_c) + shift_c

    px = hx @ w_in
    a_k, a_v, b_k, b_v, a_q, b_q, a_z, b_z, g_a, g_b = _split(px, SPLIT_SIZES)
    pc = hc @ (w_in if update_ctx else w_in[:, :KV_COLS])
    ca_k, ca_v, cb_k, cb_v = _split(pc[..., :KV_COLS], SPLIT_SIZES[:4])

    hs = lambda t, h: t.reshape(t.shape[0], t.shape[1], h, HEAD_DIM)
    qa = _rmsnorm(hs(a_q, NA_HEADS), q_norm_a)
    ka = _rmsnorm(hs(a_k, NA_HEADS), k_norm_a)
    va = hs(a_v, NA_HEADS)
    cka = _rmsnorm(hs(ca_k, NA_HEADS), k_norm_a)
    cva = hs(ca_v, NA_HEADS)
    a_att = _na_latent(qa, ka, va, cka, cva, rpb, rows)

    qb = _rope_2d(_rmsnorm(hs(b_q, GQA_Q_HEADS), q_norm_b), pos_row, pos_col)
    kb = _rope_2d(_rmsnorm(hs(b_k, GQA_KV_HEADS), k_norm_b), pos_row, pos_col)
    vb = hs(b_v, GQA_KV_HEADS)
    ckb = _rmsnorm(hs(cb_k, GQA_KV_HEADS), k_norm_b)
    cvb = hs(cb_v, GQA_KV_HEADS)
    k_all = jnp.concatenate([ckb, kb], axis=1)
    v_all = jnp.concatenate([cvb, vb], axis=1)
    b_att = _gqa_latent(qb, k_all, v_all)

    out_x = _merge(a_att, b_att, a_z, b_z, g_a, g_b, w_o_a, w_o_b, w_out)
    x_new = x + gate_x * out_x

    if update_ctx:
        _, _, _, _, c_aq, c_bq, c_az, c_bz, c_ga, c_gb = _split(pc, SPLIT_SIZES)
        cqa = _rmsnorm(hs(c_aq, NA_HEADS), q_norm_a)[:, :, :, None, :]
        c_a_att = _attend(cqa, cka, cva).reshape(B, L, NA_WIDTH)
        cqb = _rmsnorm(hs(c_bq, GQA_Q_HEADS), q_norm_b).reshape(
            B, L, GQA_KV_HEADS, GQA_GROUP, HEAD_DIM)
        c_b_att = _attend(cqb, ckb, cvb).reshape(B, L, GQA_WIDTH)
        out_c = _merge(c_a_att, c_b_att, c_az, c_bz, c_ga, c_gb, w_o_a, w_o_b, w_out)
        ctx = ctx + gate_c * out_c
    return x_new, ctx

def second_inputs(seed: int = 0) -> dict:
    key = jax.random.key(seed)
    ks = jax.random.split(key, 16)
    f32 = jnp.float32
    nrm = lambda k, shape, s: jax.random.normal(k, shape, f32) * s
    return {
        "x": nrm(ks[0], (BATCH, SEQ, D_MODEL), 1.0),
        "c": nrm(ks[1], (BATCH, D_MODEL), 1.0),
        "ctx": nrm(ks[2], (BATCH, CTX_LEN, D_MODEL), 1.0),
        "c_ctx": nrm(ks[3], (D_MODEL,), 1.0),
        "w_ada": nrm(ks[4], (DEPTH, D_MODEL, 3 * D_MODEL), D_MODEL ** -0.5),
        "b_ada": nrm(ks[5], (DEPTH, 3 * D_MODEL), 0.02),
        "norm_g": 1.0 + nrm(ks[6], (DEPTH, D_MODEL), 0.05),
        "w_in": nrm(ks[7], (DEPTH, D_MODEL, IN_COLS), D_MODEL ** -0.5),
        "q_norm_a": 1.0 + nrm(ks[8], (DEPTH, HEAD_DIM), 0.05),
        "k_norm_a": 1.0 + nrm(ks[9], (DEPTH, HEAD_DIM), 0.05),
        "q_norm_b": 1.0 + nrm(ks[10], (DEPTH, HEAD_DIM), 0.05),
        "k_norm_b": 1.0 + nrm(ks[11], (DEPTH, HEAD_DIM), 0.05),
        "rpb": nrm(ks[12], (DEPTH, NA_HEADS, 2 * WIN_R - 1, 2 * WIN_C - 1), 0.1),
        "w_o_a": nrm(ks[13], (DEPTH, NA_WIDTH, D_MODEL), NA_WIDTH ** -0.5),
        "w_o_b": nrm(ks[14], (DEPTH, GQA_WIDTH, D_MODEL), GQA_WIDTH ** -0.5),
        "w_out": nrm(ks[15], (DEPTH, D_MODEL, D_MODEL), D_MODEL ** -0.5),
    }

def second_block(x, c, ctx, c_ctx, w_ada, b_ada, norm_g, w_in, q_norm_a, k_norm_a,
              q_norm_b, k_norm_b, rpb, w_o_a, w_o_b, w_out):
    S = x.shape[1]
    t = jnp.arange(S, dtype=jnp.int32)
    pos_row = t // GRID_W
    pos_col = t % GRID_W
    for l in range(DEPTH):
        x, ctx = _layer(x, ctx, c, c_ctx, w_ada[l], b_ada[l], norm_g[l], w_in[l],
                        q_norm_a[l], k_norm_a[l], q_norm_b[l], k_norm_b[l], rpb[l],
                        w_o_a[l], w_o_b[l], w_out[l], pos_row, pos_col,
                        l < DEPTH - 1)
    return x


def setup_inputs(seed=0):
    out = dict(first_inputs(seed))
    for name, value in second_inputs(seed + 1).items():
        if name != "x":
            out[name + "_2"] = value
    return out


def reference(
    x, a_w_in, a_conv_w, a_a_log, a_dt_bias, a_norm_w, a_w_out, kv_w, b_w_q, b_lambda,
    b_subln_w, b_w_out, ln_mix_g, ln_mix_b, ln_ffn_g, ln_ffn_b, moe_w_group, moe_w_expert,
    moe_w13, moe_w2, c_2, ctx_2, c_ctx_2, w_ada_2, b_ada_2, norm_g_2, w_in_2, q_norm_a_2,
    k_norm_a_2, q_norm_b_2, k_norm_b_2, rpb_2, w_o_a_2, w_o_b_2, w_out_2,
):
    x = first_block(
        x, a_w_in, a_conv_w, a_a_log, a_dt_bias, a_norm_w, a_w_out, kv_w, b_w_q, b_lambda,
        b_subln_w, b_w_out, ln_mix_g, ln_mix_b, ln_ffn_g, ln_ffn_b, moe_w_group, moe_w_expert,
        moe_w13, moe_w2,
    )
    return second_block(
        x, c_2, ctx_2, c_ctx_2, w_ada_2, b_ada_2, norm_g_2, w_in_2, q_norm_a_2, k_norm_a_2,
        q_norm_b_2, k_norm_b_2, rpb_2, w_o_a_2, w_o_b_2, w_out_2,
    )


_drawn_inputs = setup_inputs


def setup_inputs(seed=0):
    import zlib

    import numpy as np

    out = dict(_drawn_inputs(seed))
    spreads = {}
    factors = {'a_norm_w': 6.877,
     'b_lambda': 8.0,
     'b_subln_w': 7.714,
     'b_ada_2': 3.637,
     'norm_g_2': 3.918,
     'q_norm_a_2': 8.0,
     'k_norm_a_2': 8.0,
     'q_norm_b_2': 8.0,
     'k_norm_b_2': 8.0,
     'rpb_2': 8.0}
    for name, (base, spread) in spreads.items():
        noise = np.random.default_rng([zlib.crc32(name.encode()), seed]).standard_normal(out[name].shape)
        drawn = base * np.exp(spread * noise) if base else spread * noise
        out[name] = __import__('jax').numpy.asarray(drawn.astype(out[name].dtype))
    for name, factor in factors.items():
        out[name] = (out[name] * factor).astype(out[name].dtype)
    return out
```

```python
import math
from contextlib import ExitStack

import numpy as np

import concourse.bass as bass
from concourse import mybir

F32 = mybir.dt.float32
I32 = mybir.dt.int32
U32 = mybir.dt.uint32
ACT = mybir.ActivationFunctionType
ALU = mybir.AluOpType
AX = mybir.AxisListType

P = 128
D = 1024
KD = D // P
T = 512
NT = T // P
CTX = 256
HEADS = 8
CH = 64
NCH = T // CH
LN_EPS = 1e-5
RMS_EPS = 1e-6
DEPTH = 2
ALPHA = (2 * DEPTH) ** 0.25
LAMBDA_INIT = 0.8 - 0.6 * math.exp(-0.3 * 1)
NEG = -1e30
NE = 32
NGRP = 4
EPG = 8
BLK = 64
EXTRA = 16
ROWS = (NE + EXTRA) * BLK
RING = 6
SLOT = 4096


class Steps:

    def __init__(self, sem, base, labels):
        self.sem, self.base = sem, base
        self.labels = labels
        self.index = {x: n for n, x in enumerate(labels)}
        assert len(self.index) == len(labels)
        self.next = 0

    def __call__(self, label):
        want = self.labels[self.next % len(self.labels)]
        assert want == label, f"{label} stands where {want} is due"
        self.next += 1
        return self.sem, 1

    def at(self, label, turn=0):
        return self.sem, turn * len(self.labels) + (self.base + self.index[label] + 1)

    def before(self, turn):
        assert self.base > 0
        return self.sem, turn * len(self.labels) + self.base


class Weights:

    def __init__(self, nc, name, buf, ring):
        self.buf, self.ring = buf, ring
        self.landed = [nc.alloc_semaphore(f"{name}_landed_{i}") for i in range(ring)]
        self.loads = []
        self.free = {}
        self.issued = 0
        self.used = 0

    def slot(self, n, k, w):
        return self.buf[:, n % self.ring, 0:k * w].rearrange("p (k n) -> p k n", k=k)

    def landed_at(self, n):
        same = [self.loads[i] for i in range(n % self.ring, n + 1, self.ring)]
        return self.landed[n % self.ring], 16 * sum(len(x[0]) if x and isinstance(x[0], list) else 1 for x in same)

    def issue(self, sp, upto):
        upto = min(upto, len(self.loads))
        while self.issued < upto:
            n = self.issued
            if self.loads[n] is None:
                return
            if n >= self.ring:
                sp.wait_ge(*self.free[n - self.ring])
            src, k, w = self.loads[n]
            if isinstance(src, list):
                m = w // len(src)
                for i, piece in enumerate(src):
                    sp.dma_start(self.slot(n, k, w)[:, :, i * m:(i + 1) * m], piece).then_inc(self.landed[n % self.ring], 16)
                self.issued += 1
                continue
            sp.dma_start(self.slot(n, k, w), src).then_inc(self.landed[n % self.ring], 16)
            self.issued += 1


class Kernel:
    def __init__(self, nc, A, out):
        self.nc, self.A, self.out = nc, A, out
        self.ring = nc.alloc_sbuf_tensor("weight_ring", [P, RING, SLOT], F32)
        self.w = Weights(nc, "weights", self.ring, RING)
        self.bank = nc.alloc_psum_tensor("banks", [P, 8, 512], F32)
        self.ps = [self.bank[:, i, :] for i in range(8)]
        self.counted = {n: [nc.alloc_semaphore(n), 1] for n in
                        ("dn_heads_dve", "attention_pe", "attention_dve", "attention_pool")}
        self.const = nc.alloc_sbuf_tensor("consts", [P, CONST_COLS], F32)
        self.loaded = nc.alloc_semaphore("small_loads")
        self.n_loaded = 0
        self.H = nc.alloc_sbuf_tensor("rows", [P, NT, D], F32)
        self.HT = nc.alloc_sbuf_tensor("cols", [P, KD, T], F32)
        self.OT = nc.alloc_sbuf_tensor("cols_2", [P, KD, T], F32)

    def c(self, name):
        a, b = CONSTS[name]
        return self.const[:, a:b]

    def steps(self, kind, turns=1, **engines):
        out = []
        for e, labels in engines.items():
            name = f"{kind}_{e}"
            if name not in self.counted:
                self.counted[name] = [self.nc.alloc_semaphore(name), 0]
            sem, base = self.counted[name]
            self.counted[name][1] += turns * len(labels)
            out.append(Steps(sem, base, labels))
        return out

    def load(self, eng, dst, src):
        eng.dma_start(dst, src).then_inc(self.loaded, 16)
        self.n_loaded += 16


def host_constants():
    i = np.arange(P)
    same = (i[:, None] // CH) == (i[None, :] // CH)
    c = {}
    c["ident"] = np.eye(P)
    c["ones"] = np.ones((P, P))
    c["cum"] = same & (i[:, None] <= i[None, :])
    c["strict_cols"] = same & (i[None, :] < i[:, None])
    c["causal_neg"] = np.where(same & (i[:, None] <= i[None, :]), 0.0, NEG)
    for lev in range(6):
        s = 1 << lev
        low = (i[:, None] // (2 * s) == i[None, :] // (2 * s)) & (i[:, None] // s % 2 == 1) & (i[None, :] // s % 2 == 0)
        c[f"low{lev}"] = low
        c[f"lowT{lev}"] = low.T
    c["before"] = i[:, None] < i[None, :]
    c["half_ones"] = (i[:, None] // 64) == (i[None, :] // 64)
    c["tril_neg"] = np.where(i[None, :] <= i[:, None], 0.0, NEG)
    qc = i % 64
    start = np.clip(qc - 8, 0, 64 - 16)
    kc = np.arange(64)[None, :]
    c["win_neg"] = np.where((kc >= start[:, None]) & (kc < start[:, None] + 16), 0.0, NEG)
    c["swap"] = i[:, None] == (i[None, :] ^ 16)
    c["eps"] = np.tile(np.array([[RMS_EPS, LN_EPS, 1.0, 0.0]]), (P, 1))
    c["iota32"] = np.tile(np.arange(32), (P, 1))
    c["group32"] = np.tile(np.arange(32) // EPG, (P, 1))
    c["iota16"] = np.tile(np.arange(16), (P, 1))
    c["multiple8"] = np.tile(np.arange(8) * BLK, (P, 1))
    c["base32"] = np.tile(np.arange(32) * BLK, (P, 1))
    cols, at = {}, 0
    for k, v in c.items():
        cols[k] = (at, at + v.shape[1])
        at += v.shape[1]
    return cols, np.concatenate([np.asarray(v, np.float32) for v in c.values()], axis=1)


CONSTS, CONST_ARRAY = host_constants()
CONST_COLS = CONST_ARRAY.shape[1]


def bc(ap, n):
    return ap.unsqueeze(len(ap.shape)).to_broadcast(list(ap.shape) + [n])


def bm(ap, n):
    return ap.unsqueeze(1).to_broadcast([ap.shape[0], n] + list(ap.shape[1:]))



def stage_to_cols(K, name, src, dst, nt, kd=KD, scale=None, shift=None):
    nc, ps = K.nc, K.ps
    E, S, V = K.steps("cols", pe=[f"t{k}" for k in range(kd)], act=[f"c{k}" for k in range(0, kd, 2)],
                      dve=[f"c{k}" for k in range(1, kd, 2)])
    ident = K.c("ident")
    w = nt * P
    with nc.Block() as block:
        @block.sync
        def _(sp):
            K.w.issue(sp, K.w.used + K.w.ring)

        @block.tensor
        def _(pe):
            for k in range(kd):
                for t in range(nt):
                    mm = pe.transpose(ps[k][:, t * P:(t + 1) * P], src[:, t, k * P:(k + 1) * P], ident)
                mm.then_inc(*E(f"t{k}"))

        @block.scalar
        def _(act):
            for k in range(0, kd, 2):
                act.wait_ge(*E.at(f"t{k}"))
                if scale is None:
                    act.activation(dst[:, k, 0:w], ps[k][:, 0:w], ACT.Copy).then_inc(*S(f"c{k}"))
                else:
                    act.activation(dst[:, k, 0:w], ps[k][:, 0:w], ACT.Identity, scale=scale[:, k:k + 1],
                                   bias=shift[:, k:k + 1]).then_inc(*S(f"c{k}"))

        @block.vector
        def _(dve):
            for k in range(1, kd, 2):
                dve.wait_ge(*E.at(f"t{k}"))
                if scale is None:
                    dve.tensor_copy(dst[:, k, 0:w], ps[k][:, 0:w]).then_inc(*V(f"c{k}"))
                else:
                    dve.tensor_scalar(dst[:, k, 0:w], ps[k][:, 0:w], scale[:, k:k + 1], shift[:, k:k + 1],
                                      ALU.mult, ALU.add).then_inc(*V(f"c{k}"))


def plan_gemm(K, W, c0, width, kd):
    K.w.loads.append((W.rearrange("(k p) n -> p k n", p=P)[:, :, c0:c0 + width], kd, width))


def stage_gemm(K, name, groups, xT, nt, on_act, on_dve, ahead=None, extra_sp=None):
    nc, ps = K.nc, K.ps
    units = []
    for g, (mode, kd, width) in enumerate(groups):
        if mode == "rows":
            for c in range(0, width, 512):
                units += [(g, mode, t, c, min(512, width - c)) for t in range(nt)]
        else:
            units += [(g, mode, c, 0, nt * P) for c in range(width // P)]
    n0 = K.w.used
    to_act = [i for i in range(len(units)) if i % 2 == 0 and on_act is not None]
    to_dve = [i for i in range(len(units)) if i not in to_act]
    E, S, V = K.steps("product", pe=[f"u{i}" for i in range(len(units))], act=[f"e{i}" for i in to_act],
                      dve=[f"e{i}" for i in to_dve])
    for i, u in enumerate(units):
        K.w.free[n0 + u[0]] = E.at(f"u{i}")
    K.w.used = n0 + len(groups)
    with nc.Block() as block:
        @block.sync
        def _(sp):
            K.w.issue(sp, K.w.used + (ahead or K.w.ring))
            if extra_sp:
                extra_sp(sp, S, V)

        @block.tensor
        def _(pe):
            seen = -1
            for i, (g, mode, j, c, wd) in enumerate(units):
                kd, width = groups[g][1:]
                w = K.w.slot(n0 + g, kd, width)
                if g != seen:
                    pe.wait_ge(*K.w.landed_at(n0 + g))
                    seen = g
                if i >= 8:
                    pe.wait_ge(*(S if i - 8 in to_act else V).at(f"e{i - 8}"))
                for k in range(kd):
                    if mode == "rows":
                        mm = pe.matmul(ps[i % 8][:, 0:wd], xT[:, k, j * P:(j + 1) * P], w[:, k, c:c + wd],
                                       start=k == 0, stop=k == kd - 1)
                    else:
                        mm = pe.matmul(ps[i % 8][:, 0:wd], w[:, k, j * P:(j + 1) * P], xT[:, k, 0:wd],
                                       start=k == 0, stop=k == kd - 1)
                mm.then_inc(*E(f"u{i}"))

        @block.scalar
        def _(act):
            for i in to_act:
                act.wait_ge(*E.at(f"u{i}"))
                on_act(act, units[i], ps[i % 8][:, 0:units[i][4]], S(f"e{i}"))

        @block.vector
        def _(dve):
            for i in to_dve:
                dve.wait_ge(*E.at(f"u{i}"))
                on_dve(dve, units[i], ps[i % 8][:, 0:units[i][4]], V(f"e{i}"))


def stage_layer_norm(K, name, X, g_dram, b_dram):
    nc = K.nc
    with ExitStack() as mem:
        gb = mem.enter_context(nc.sbuf_tensor(f"{name}_gb", [P, 2, D], F32))
        st = mem.enter_context(nc.sbuf_tensor(f"{name}_st", [P, NT, 2, 6], F32))
        mv = mem.enter_context(nc.sbuf_tensor(f"{name}_mv", [P, NT, 2], F32))
        rs = mem.enter_context(nc.sbuf_tensor(f"{name}_rs", [P, NT], F32))
        V, S = K.steps("layer_norm", dve=[f"{x}{t}" for t in range(NT) for x in ("st0", "st1", "mv")]
                          + [f"{x}{t}" for t in range(NT) for x in ("nb", "sc", "g")],
                          act=["ln", "rs"])
        with nc.Block() as block:
            @block.sync
            def _(sp):
                K.load(sp, gb[:, 0, :], g_dram.partition_broadcast(P))
                K.load(sp, gb[:, 1, :], b_dram.partition_broadcast(P))
                K.w.issue(sp, K.w.used + K.w.ring)

            @block.vector
            def _(dve):
                for t in range(NT):
                    dve.bn_stats(st[:, t, 0, :], X[:, t, 0:512]).then_inc(*V(f"st0{t}"))
                    dve.bn_stats(st[:, t, 1, :], X[:, t, 512:1024]).then_inc(*V(f"st1{t}"))
                    dve.wait_ge(*V.at(f"st1{t}"))
                    dve.bn_aggr(mv[:, t, :], st[:, t, :, :]).then_inc(*V(f"mv{t}"))
                dve.wait_ge(K.loaded, K.n_loaded)
                for t in range(NT):
                    dve.wait_ge(*S.at("rs"))
                    dve.tensor_scalar(X[:, t, :], X[:, t, :], mv[:, t, 0:1], rs[:, t:t + 1], ALU.subtract,
                                      ALU.mult).then_inc(*V(f"nb{t}"))
                    dve.wait_ge(*V.at(f"nb{t}"))
                    dve.tensor_tensor(X[:, t, :], X[:, t, :], gb[:, 0, :], ALU.mult).then_inc(*V(f"sc{t}"))
                    dve.wait_ge(*V.at(f"sc{t}"))
                    dve.tensor_tensor(X[:, t, :], X[:, t, :], gb[:, 1, :], ALU.add).then_inc(*V(f"g{t}"))

            @block.scalar
            def _(act):
                act.wait_ge(*V.at(f"mv{NT - 1}"))
                act.activation(rs[:, :], mv[:, :, 1], ACT.Ln, bias=K.c("eps")[:, 1:2]).then_inc(*S("ln"))
                act.wait_ge(*S.at("ln"))
                act.activation(rs[:, :], rs[:, :], ACT.Exp, scale=-0.5).then_inc(*S("rs"))



def stage_start(K):
    with K.nc.Block() as block:
        @block.sync
        def _(sp):
            K.load(sp, K.const[:, :], K.A["consts"])
            K.load(sp, K.H[:, :, :], K.A["x"][0].rearrange("(t p) d -> p t d", p=P))
            for sem, one in K.counted.values():
                sp.sem_inc(sem, one)
            K.w.issue(sp, RING)
            sp.wait_ge(K.loaded, K.n_loaded)


def plan_dn_projection(K):
    for g in range(8):
        plan_gemm(K, K.A["a_w_in"][0], 512 * g, 512, KD)


def stage_dn_projection(K, proj):
    nc = K.nc
    stored = [nc.alloc_semaphore(f"proj_stored_{i}") for i in range(8)]
    with ExitStack() as mem:
        buf = mem.enter_context(nc.sbuf_tensor("proj_out", [P, 8, 512], F32))

        def chunk(u):
            return 4 * u[0] + u[2]

        def take_act(act, u, bank, inc):
            c = chunk(u)
            if c >= 8:
                act.wait_ge(stored[c % 8], 16 * (c // 8))
            act.activation(buf[:, c % 8, :], bank, ACT.Copy).then_inc(*inc)

        def take_dve(dve, u, bank, inc):
            c = chunk(u)
            if c >= 8:
                dve.wait_ge(stored[c % 8], 16 * (c // 8))
            dve.tensor_copy(buf[:, c % 8, :], bank).then_inc(*inc)

        def store(sp, S, V):
            for c in range(32):
                sp.wait_ge(*(V if c % 2 else S).at(f"e{c}"))
                sp.dma_start(proj[c], buf[:, c % 8, :]).then_inc(stored[c % 8], 16)
            for i in range(8):
                sp.wait_ge(stored[i], 16 * 4)

        stage_gemm(K, "dn_projection", [("cols", KD, 512)] * 8, K.HT, NT, take_act, take_dve, ahead=2, extra_sp=store)


def stage_dn_gates(K, PH):
    nc, ps, A = K.nc, K.ps, K.A
    with ExitStack() as mem:
        wg = mem.enter_context(nc.sbuf_tensor("gate_w", [P, KD, 16], F32))
        par = mem.enter_context(nc.sbuf_tensor("gate_par", [P, 2, HEADS], F32))
        a = mem.enter_context(nc.sbuf_tensor("gate_a", [P, NT, HEADS], F32))
        b = mem.enter_context(nc.sbuf_tensor("gate_b", [P, NT, HEADS], F32))
        e = mem.enter_context(nc.sbuf_tensor("gate_e", [P, NT, HEADS], F32))
        E, S, V = K.steps("dn_gates", pe=["logits", "cum"], act=["eb", "ea", "exp", "ln", "egc"],
                          dve=["b1", "beta", "a", "abs", "e1", "pos", "sp", "neg", "g", "gc", "beg"])
        logit = ps[0][:, 0:NT * 16].rearrange("p (t c) -> p t c", c=16)
        cum = ps[1][:, 0:NT * HEADS]
        with nc.Block() as block:
            @block.sync
            def _(sp):
                with nc.allow_non_contiguous_dma(reason="16 columns of the projection"):
                    K.load(sp, wg[:, :, :], A["a_w_in"][0].rearrange("(k p) n -> p k n", p=P)[:, :, 4096:4112])
                K.load(sp, par[:, 0, :], A["a_a_log"][0].partition_broadcast(P))
                K.load(sp, par[:, 1, :], A["a_dt_bias"][0].partition_broadcast(P))
                K.w.issue(sp, K.w.used + 2)

            @block.tensor
            def _(pe):
                pe.wait_ge(K.loaded, K.n_loaded)
                for t in range(NT):
                    for k in range(KD):
                        mm = pe.matmul(ps[0][:, t * 16:(t + 1) * 16], K.HT[:, k, t * P:(t + 1) * P], wg[:, k, :],
                                       start=k == 0, stop=k == KD - 1)
                mm.then_inc(*E("logits"))
                pe.wait_ge(*V.at("g"))
                pe.matmul(cum, K.c("cum"), PH[:, 1, :, :].rearrange("p t h -> p (t h)"), start=True,
                          stop=True).then_inc(*E("cum"))

            @block.scalar
            def _(act):
                act.wait_ge(*E.at("logits"))
                act.activation(b[:, :, :], logit[:, :, 0:8], ACT.Exp, scale=-1.0).then_inc(*S("eb"))
                act.activation(par[:, 0, :], par[:, 0, :], ACT.Exp).then_inc(*S("ea"))
                act.wait_ge(*V.at("abs"))
                act.activation(e[:, :, :], e[:, :, :], ACT.Exp).then_inc(*S("exp"))
                act.wait_ge(*V.at("e1"))
                act.activation(e[:, :, :], e[:, :, :], ACT.Ln).then_inc(*S("ln"))
                act.wait_ge(*V.at("gc"))
                act.activation(e[:, :, :], PH[:, 2, :, :], ACT.Exp).then_inc(*S("egc"))

            @block.vector
            def _(dve):
                dve.wait_ge(*S.at("eb"))
                dve.tensor_scalar(b[:, :, :], b[:, :, :], 1.0, None, ALU.add).then_inc(*V("b1"))
                dve.wait_ge(*V.at("b1"))
                dve.reciprocal(PH[:, 0, :, :], b[:, :, :]).then_inc(*V("beta"))
                dve.tensor_tensor(a[:, :, :], logit[:, :, 8:16], bm(par[:, 1, :], NT), ALU.add).then_inc(*V("a"))
                dve.wait_ge(*V.at("a"))
                dve.scalar_tensor_tensor(e[:, :, :], a[:, :, :], -1.0, a[:, :, :], ALU.mult, ALU.min).then_inc(*V("abs"))
                dve.wait_ge(*S.at("exp"))
                dve.tensor_scalar(e[:, :, :], e[:, :, :], 1.0, None, ALU.add).then_inc(*V("e1"))
                dve.tensor_scalar(a[:, :, :], a[:, :, :], 0.0, None, ALU.max).then_inc(*V("pos"))
                dve.wait_ge(*V.at("pos"))
                dve.wait_ge(*S.at("ln"))
                dve.tensor_tensor(a[:, :, :], a[:, :, :], e[:, :, :], ALU.add).then_inc(*V("sp"))
                dve.tensor_scalar(par[:, 0, :], par[:, 0, :], -1.0, None, ALU.mult).then_inc(*V("neg"))
                dve.wait_ge(*V.at("neg"))
                dve.tensor_tensor(PH[:, 1, :, :], a[:, :, :], bm(par[:, 0, :], NT), ALU.mult).then_inc(*V("g"))
                dve.wait_ge(*E.at("cum"))
                dve.tensor_copy(PH[:, 2, :, :], cum.rearrange("p (t h) -> p t h", h=8)).then_inc(*V("gc"))
                dve.wait_ge(*S.at("egc"))
                dve.tensor_tensor(PH[:, 3, :, :], e[:, :, :], PH[:, 0, :, :], ALU.mult).then_inc(*V("beg"))


def stage_dn_heads(K, proj, PH, M):
    nc, ps, A = K.nc, K.ps, K.A
    u_k, wT_k, qd_k, at_k, kd_k = range(5)
    with ExitStack() as mem:
        spare, at = K.w.buf[:, 4:6, :].rearrange("p a n -> p (a n)"), [0]

        def sb(n, shape):
            size = math.prod(shape[1:])
            got = spare[0:shape[0], at[0]:at[0] + size]
            at[0] += size
            return got.rearrange("p (a b) -> p a b", a=shape[1]) if len(shape) == 3 else got
        cwr = sb("cwr", [96, P])
        cw = sb("cw", [P, 96])
        cwh = sb("cwh", [P, 12])
        ph = sb("ph", [P, 4, NT])
        raw = sb("raw", [P, 3, T + 3])
        qkv = sb("qkv", [P, 3, T])
        sq = sb("sq", [P, 2, T])
        gm = sb("gm", [P, 2, T])
        dec = sb("dec", [P, T])
        AT = sb("AT", [P, T])
        X = sb("X", [P, T])
        XT = sb("XT", [P, T])
        kds = sb("kds", [P, NT])
        Pm = gm[:, 0, :]
        vb = sq[:, 0, :]
        kbg = sq[:, 1, :]
        tmp = gm[:, 1, :]
        GL, M = M["GL"], M["M"]
        lev = range(1, 6)
        E, S, V = K.steps(
            "dn_heads", turns=HEADS,
            pe=["ssq", "gcb", "bet", "kk", "qk", "kr", "vr", "P0"] + [f"{x}{n}" for n in lev for x in ("P", "D", "T")
                                                                     if not (x == "D" and n == 5)] + ["u", "w"],
            act=["silu", "sqr", "ln", "rs", "eg", "exd", "kds"] + [f"p{n}" for n in lev] + ["u", "w"],
            dve=["ph", "cwh"] + [f"c{w}{j}" for w in range(3) for j in range(4)] + ["mg", "mb", "qn", "kn",
                 "diff", "neg", "kd0", "kd1", "gl", "at", "A0", "AT", "vb", "kbg", "kdec", "qd", "m0", "x0", "m0t", "x0t"]
            + [f"{x}{n}" for n in lev for x in ("m", "x", "mt", "xt") if not (n == 5 and x in ("m", "x"))])
        got = nc.alloc_semaphore("dn_head_loaded")
        got_cw = nc.alloc_semaphore("conv_w_loaded")
        cw_t = nc.alloc_semaphore("conv_w_turned")
        zero = nc.alloc_semaphore("conv_pad_zero")

        def t3(x):
            return x.rearrange("p (t n) -> p t n", t=NT)

        with nc.Block() as block:
            @block.sync
            def _(sp):
                sp.dma_start(cwr[:, :], A["a_conv_w"][0].rearrange("j (c p) -> (j c) p", p=P)).then_inc(got_cw, 16)
                with sp.Fori(0, HEADS) as h:
                    sp.wait_ge(*V.before(h))
                    sp.dma_start(raw[:, :, 3:T + 3], proj[0:24].rearrange("(w h) p t -> p w h t", h=HEADS)
                                 [:, :, bass.ds(h, 1), :].rearrange("p w h t -> p (w h) t")).then_inc(got, 16)
                K.w.issue(sp, K.w.used + 2)

            @block.tensor
            def _(pe):
                pe.wait_ge(got_cw, 16)
                pe.transpose(ps[0][:, 0:96], cwr[:, :], K.c("ident")[0:96, 0:96]).then_inc(cw_t, 1)
                with pe.Fori(0, HEADS) as h:
                    pe.wait_ge(*S.at("sqr", h))
                    pe.wait_ge(*V.at("ph", h))
                    for w in range(2):
                        mm = pe.matmul(ps[w][:, :], K.c("ones"), sq[:, w, :], start=True, stop=True)
                    mm.then_inc(*E("ssq"))
                    pe.wait_ge(*V.at("mg", h))
                    pe.matmul(ps[6][:, :], K.c("ones"), gm[:, 0, :], start=True, stop=True).then_inc(*E("gcb"))
                    pe.wait_ge(*V.at("mb", h))
                    pe.matmul(ps[7][:, :], K.c("strict_cols"), gm[:, 1, :], start=True, stop=True).then_inc(*E("bet"))
                    pe.wait_ge(*V.at("kn", h))
                    for t in range(NT):
                        c = slice(t * P, (t + 1) * P)
                        mm = pe.matmul(ps[2][:, c], qkv[:, 1, c], qkv[:, 1, c], start=True, stop=True)
                    mm.then_inc(*E("kk"))
                    for t in range(NT):
                        c = slice(t * P, (t + 1) * P)
                        mm = pe.matmul(ps[3][:, c], qkv[:, 1, c], qkv[:, 0, c], start=True, stop=True)
                    mm.then_inc(*E("qk"))
                    for n, w in ((4, 1), (5, 2)):
                        for t in range(NT):
                            c = slice(t * P, (t + 1) * P)
                            mm = pe.transpose(ps[n][:, c], qkv[:, w, c], K.c("ident"))
                        mm.then_inc(*E("kr" if n == 4 else "vr"))
                    pe.wait_ge(*V.at("AT", h))
                    for t in range(NT):
                        c = slice(t * P, (t + 1) * P)
                        mm = pe.transpose(ps[0][:, c], AT[:, c], K.c("ident"))
                    mm.then_inc(*E("P0"))
                    for n in lev:
                        pe.wait_ge(*V.at("x0t" if n == 1 else f"xt{n - 1}", h))
                        for t in range(NT):
                            c = slice(t * P, (t + 1) * P)
                            mm = pe.matmul(ps[0][:, c], AT[:, c], X[:, c], start=True, stop=True)
                        mm.then_inc(*E(f"P{n}"))
                        pe.wait_ge(*S.at(f"p{n}", h))
                        if n < 5:
                            for t in range(NT):
                                c = slice(t * P, (t + 1) * P)
                                mm = pe.matmul(ps[1][:, c], XT[:, c], Pm[:, c], start=True, stop=True)
                            mm.then_inc(*E(f"D{n}"))
                        for t in range(NT):
                            c = slice(t * P, (t + 1) * P)
                            mm = pe.matmul(ps[2][:, c], Pm[:, c], XT[:, c], start=True, stop=True)
                        mm.then_inc(*E(f"T{n}"))
                    pe.wait_ge(*V.at("xt5", h))
                    for t in range(NT):
                        c = slice(t * P, (t + 1) * P)
                        mm = pe.matmul(ps[3][:, c], XT[:, c], vb[:, c], start=True, stop=True)
                    mm.then_inc(*E("u"))
                    for t in range(NT):
                        c = slice(t * P, (t + 1) * P)
                        mm = pe.matmul(ps[4][:, c], kbg[:, c], XT[:, c], start=True, stop=True)
                    mm.then_inc(*E("w"))

            @block.scalar
            def _(act):
                with act.Fori(0, HEADS) as h:
                    act.wait_ge(*V.at("c23", h))
                    act.activation(qkv[:, :, :], qkv[:, :, :], ACT.Silu).then_inc(*S("silu"))
                    act.wait_ge(*S.at("silu", h))
                    act.activation(sq[:, :, :], qkv[:, 0:2, :], ACT.Square).then_inc(*S("sqr"))
                    act.wait_ge(*E.at("ssq", h))
                    for w in range(2):
                        i = act.activation(sq[:, w, :], ps[w][:, :], ACT.Ln, bias=K.c("eps")[:, 0:1])
                    i.then_inc(*S("ln"))
                    act.wait_ge(*S.at("ln", h))
                    act.activation(sq[:, :, :], sq[:, :, :], ACT.Exp, scale=-0.5).then_inc(*S("rs"))
                    act.wait_ge(*E.at("gcb", h))
                    act.activation(dec[:, :], ps[6][:, :], ACT.Exp).then_inc(*S("eg"))
                    act.wait_ge(*V.at("neg", h))
                    act.activation(AT[:, :], AT[:, :], ACT.Exp).then_inc(*S("exd"))
                    act.wait_ge(*V.at("kd1", h))
                    act.activation(kds[:, :], kds[:, :], ACT.Exp).then_inc(*S("kds"))
                    for n in lev:
                        act.wait_ge(*E.at(f"P{n}", h))
                        act.activation(Pm, ps[0][:, :], ACT.Copy).then_inc(*S(f"p{n}"))
                    act.wait_ge(*E.at("u", h))
                    act.activation(M[u_k][:, bass.ds(h, 1), :].rearrange("p a n -> p (a n)"), ps[3][:, :], ACT.Copy).then_inc(*S("u"))
                    act.wait_ge(*E.at("w", h))
                    act.activation(M[wT_k][:, bass.ds(h, 1), :].rearrange("p a n -> p (a n)"), ps[4][:, :], ACT.Copy).then_inc(*S("w"))

            @block.vector
            def _(dve):
                dve.memset(raw[:, :, 0:3], 0.0).then_inc(zero, 1)
                dve.wait_ge(cw_t, 1)
                dve.tensor_copy(cw[:, :], ps[0][:, 0:96]).then_inc(zero, 1)
                dve.wait_ge(zero, 2)
                with dve.Fori(0, HEADS) as h:
                    dve.tensor_copy(ph[:, :, :], PH[:, :, :, bass.ds(h, 1)].rearrange("p a t h -> p a (t h)")).then_inc(*V("ph"))
                    dve.tensor_copy(cwh[:, :], cw[:, :].rearrange("p (a h) -> p a h", h=HEADS)[:, :, bass.ds(h, 1)]
                                    .rearrange("p a h -> p (a h)")).then_inc(*V("cwh"))
                    dve.wait_ge(*V.at("cwh", h))
                    dve.wait_ge(got, 16 * h + 16)
                    for w in range(3):
                        dve.tensor_scalar(qkv[:, w, :], raw[:, w, 0:T], cwh[:, w:w + 1], None, ALU.mult).then_inc(*V(f"c{w}0"))
                        for j in range(1, 4):
                            dve.wait_ge(*V.at(f"c{w}{j - 1}", h))
                            dve.scalar_tensor_tensor(qkv[:, w, :], raw[:, w, j:T + j], cwh[:, 3 * j + w:3 * j + w + 1],
                                                     qkv[:, w, :], ALU.mult, ALU.add).then_inc(*V(f"c{w}{j}"))
                    dve.tensor_tensor(t3(gm[:, 0, :]), bm(K.c("cum"), NT), bc(ph[:, 1, :], P), ALU.mult).then_inc(*V("mg"))
                    dve.tensor_tensor(t3(gm[:, 1, :]), bm(K.c("ident"), NT), bc(ph[:, 0, :], P), ALU.mult).then_inc(*V("mb"))
                    dve.wait_ge(*S.at("rs", h))
                    dve.scalar_tensor_tensor(qkv[:, 0, :], qkv[:, 0, :], float(P) ** -0.5, sq[:, 0, :], ALU.mult,
                                             ALU.mult).then_inc(*V("qn"))
                    dve.tensor_tensor(qkv[:, 1, :], qkv[:, 1, :], sq[:, 1, :], ALU.mult).then_inc(*V("kn"))
                    dve.wait_ge(*S.at("eg", h))
                    dve.tensor_tensor(t3(AT[:, :]), t3(ps[6][:, :]), bc(ph[:, 2, :], P), ALU.subtract).then_inc(*V("diff"))
                    dve.wait_ge(*V.at("diff", h))
                    dve.tensor_tensor(t3(AT[:, :]), t3(AT[:, :]), bm(K.c("causal_neg"), NT), ALU.add).then_inc(*V("neg"))
                    for half in range(2):
                        r = slice(64 * half, 64 * half + 64)
                        dve.tensor_tensor(kds[r, :], t3(ps[6][:, :])[r, :, 64 * half + 63], ph[r, 2, :],
                                          ALU.subtract).then_inc(*V(f"kd{half}"))
                    dve.tensor_copy(GL[:, bass.ds(h, 1), :].rearrange("p a n -> p (a n)"),
                                    dec[:, :].rearrange("p (c n) -> p c n", n=CH)[:, :, CH - 1]).then_inc(*V("gl"))
                    dve.wait_ge(*S.at("exd", h))
                    dve.wait_ge(*E.at("qk", h))
                    dve.tensor_tensor(M[at_k][:, bass.ds(h, 1), :].rearrange("p a n -> p (a n)"), ps[3][:, :], AT[:, :],
                                      ALU.mult).then_inc(*V("at"))
                    dve.tensor_tensor(AT[:, :], ps[2][:, :], AT[:, :], ALU.mult).then_inc(*V("A0"))
                    dve.wait_ge(*V.at("A0", h))
                    dve.wait_ge(*E.at("bet", h))
                    dve.tensor_tensor(AT[:, :], ps[7][:, :], AT[:, :], ALU.mult).then_inc(*V("AT"))
                    dve.wait_ge(*E.at("vr", h))
                    dve.tensor_tensor(t3(vb), t3(ps[5][:, :]), bc(ph[:, 0, :], P), ALU.mult).then_inc(*V("vb"))
                    dve.tensor_tensor(t3(kbg), t3(ps[4][:, :]), bc(ph[:, 3, :], P), ALU.mult).then_inc(*V("kbg"))
                    dve.wait_ge(*S.at("kds", h))
                    dve.tensor_tensor(M[kd_k][:, bass.ds(h, 1), :].rearrange("p a (t n) -> p (a t) n", t=NT), t3(ps[4][:, :]),
                                      bc(kds[:, :], P), ALU.mult).then_inc(*V("kdec"))
                    dve.tensor_tensor(M[qd_k][:, bass.ds(h, 1), :].rearrange("p a n -> p (a n)"), qkv[:, 0, :], dec[:, :],
                                      ALU.mult).then_inc(*V("qd"))
                    dve.wait_ge(*E.at("P0", h))
                    dve.tensor_tensor(t3(X[:, :]), t3(ps[0][:, :]), bm(K.c("low0"), NT), ALU.mult).then_inc(*V("m0"))
                    dve.wait_ge(*V.at("m0", h))
                    dve.tensor_tensor(t3(X[:, :]), bm(K.c("ident"), NT), t3(X[:, :]), ALU.subtract).then_inc(*V("x0"))
                    dve.tensor_tensor(t3(XT[:, :]), t3(AT[:, :]), bm(K.c("lowT0"), NT), ALU.mult).then_inc(*V("m0t"))
                    dve.wait_ge(*V.at("m0t", h))
                    dve.tensor_tensor(t3(XT[:, :]), bm(K.c("ident"), NT), t3(XT[:, :]), ALU.subtract).then_inc(*V("x0t"))
                    for n in lev:
                        if n < 5:
                            dve.wait_ge(*E.at(f"D{n}", h))
                            dve.tensor_tensor(t3(tmp), t3(ps[1][:, :]), bm(K.c(f"low{n}"), NT), ALU.mult).then_inc(*V(f"m{n}"))
                            dve.wait_ge(*V.at(f"m{n}", h))
                            dve.tensor_tensor(X[:, :], X[:, :], tmp, ALU.subtract).then_inc(*V(f"x{n}"))
                        dve.wait_ge(*E.at(f"T{n}", h))
                        dve.tensor_tensor(t3(dec[:, :]), t3(ps[2][:, :]), bm(K.c(f"lowT{n}"), NT), ALU.mult).then_inc(*V(f"mt{n}"))
                        dve.wait_ge(*V.at(f"mt{n}", h))
                        dve.tensor_tensor(XT[:, :], XT[:, :], dec[:, :], ALU.subtract).then_inc(*V(f"xt{n}"))


def stage_dn_recurrence(K, Md, OT):
    nc, ps = K.nc, K.ps
    u_k, wT_k, qd_k, at_k, kd_k = range(5)
    M, GL = Md["M"], Md["GL"]
    with ExitStack() as mem:
        S0, Sg, vn = (K.w.buf[:, 4:6, :].rearrange("p a n -> p (a n)")[:, 1024 * i:1024 * (i + 1)]
                      .rearrange("p (h n) -> p h n", h=HEADS) for i in range(3))
        ch = range(NCH)
        E, S, V = K.steps("dn_recurrence", pe=[f"{x}{c}" for c in ch for x in ("w0", "w1", "o", "s0", "s1")],
                          act=[f"o{c}" for c in ch],
                          dve=["zero"] + [f"{x}{c}" for c in ch for x in ("v0", "v1", "g0", "g1", "s0", "s1")])
        with nc.Block() as block:
            @block.sync
            def _(sp):
                K.w.issue(sp, K.w.used + 2)

            @block.tensor
            def _(pe):
                for c in ch:
                    t, o = c // 2, 64 * (c % 2)
                    r, col = slice(o, o + 64), slice(t * P + o, t * P + o + 64)
                    pe.wait_ge(*(V.at("zero") if c == 0 else V.at(f"s1{c - 1}")))
                    for b in range(2):
                        for h in range(4 * b, 4 * b + 4):
                            mm = pe.matmul(ps[b][r, (h % 4) * P:(h % 4 + 1) * P], M[wT_k][:, h, col], S0[:, h, :],
                                           start=True, stop=True)
                        mm.then_inc(*E(f"w{b}{c}"))
                    pe.wait_ge(*V.at(f"v1{c}"))
                    if c >= 2:
                        pe.wait_ge(*S.at(f"o{c - 2}"))
                    ob = ps[2 + c % 2]
                    for h in range(HEADS):
                        pe.matmul(ob[:, h * 64:(h + 1) * 64], S0[:, h, :], M[qd_k][:, h, col], start=True, stop=False)
                        mm = pe.matmul(ob[:, h * 64:(h + 1) * 64], vn[r, h, :], M[at_k][r, h, col], start=False,
                                       stop=True)
                    mm.then_inc(*E(f"o{c}"))
                    for b in range(2):
                        for h in range(4 * b, 4 * b + 4):
                            mm = pe.matmul(ps[4 + b][:, (h % 4) * P:(h % 4 + 1) * P],
                                           M[kd_k][r, h, t * P:(t + 1) * P], vn[r, h, :], start=True, stop=True)
                        mm.then_inc(*E(f"s{b}{c}"))

            @block.scalar
            def _(act):
                for c in ch:
                    act.wait_ge(*E.at(f"o{c}"))
                    act.activation(OT[:, :, c * CH:(c + 1) * CH], ps[2 + c % 2][:, :].rearrange("p (h n) -> p h n", h=8),
                                   ACT.Copy).then_inc(*S(f"o{c}"))

            @block.vector
            def _(dve):
                dve.memset(S0[:, :, :], 0.0).then_inc(*V("zero"))
                for c in ch:
                    t, o = c // 2, 64 * (c % 2)
                    r = slice(o, o + 64)
                    for b in range(2):
                        hs = slice(4 * b, 4 * b + 4)
                        dve.wait_ge(*E.at(f"w{b}{c}"))
                        dve.tensor_tensor(vn[r, hs, :], M[u_k][r, hs, t * P:(t + 1) * P],
                                          ps[b][r, :].rearrange("p (h n) -> p h n", h=4), ALU.subtract).then_inc(*V(f"v{b}{c}"))
                    for b in range(2):
                        hs = slice(4 * b, 4 * b + 4)
                        if c == 0:
                            dve.wait_ge(*V.at("zero"))
                        else:
                            dve.wait_ge(*V.at(f"s1{c - 1}"))
                        dve.tensor_tensor(Sg[:, hs, :], S0[:, hs, :], bc(GL[:, hs, c], P), ALU.mult).then_inc(*V(f"g{b}{c}"))
                    for b in range(2):
                        hs = slice(4 * b, 4 * b + 4)
                        dve.wait_ge(*E.at(f"s{b}{c}"))
                        dve.wait_ge(*V.at(f"g{b}{c}"))
                        dve.tensor_tensor(S0[:, hs, :], Sg[:, hs, :], ps[4 + b][:, :].rearrange("p (h n) -> p h n", h=4),
                                          ALU.add).then_inc(*V(f"s{b}{c}"))


def stage_dn_output_norm(K, proj, OT):
    nc, ps, A = K.nc, K.ps, K.A
    with ExitStack() as mem:
        z = mem.enter_context(nc.sbuf_tensor("z", [P, HEADS, T], F32))
        sq = mem.enter_context(nc.sbuf_tensor("osq", [P, HEADS, T], F32))
        nw = mem.enter_context(nc.sbuf_tensor("norm_w", [P, 1], F32))
        hd = range(HEADS)
        E, S, V = K.steps("dn_output_norm", pe=[f"s{h}" for h in hd],
                          act=[f"q{h}" for h in hd] + [f"{x}{h}" for h in hd for x in ("l", "e")] + [f"z{h}" for h in hd],
                          dve=[f"{x}{h}" for h in hd for x in ("n", "z")])
        with nc.Block() as block:
            @block.sync
            def _(sp):
                K.load(sp, z[:, :, :], proj.rearrange("c p t -> p c t")[:, 24:32, :])
                K.load(sp, nw[:, :], A["a_norm_w"].rearrange("a p -> p a"))
                K.load(sp, K.H[:, :, :], K.A["x"][0].rearrange("(t p) d -> p t d", p=P))
                K.w.issue(sp, K.w.used + K.w.ring)

            @block.tensor
            def _(pe):
                for h in hd:
                    pe.wait_ge(*S.at(f"q{h}"))
                    pe.matmul(ps[h][:, :], K.c("ones"), sq[:, h, :], start=True, stop=True).then_inc(*E(f"s{h}"))

            @block.scalar
            def _(act):
                for h in hd:
                    act.activation(sq[:, h, :], OT[:, h, :], ACT.Square).then_inc(*S(f"q{h}"))
                for h in hd:
                    act.wait_ge(*E.at(f"s{h}"))
                    act.activation(sq[:, h, :], ps[h][:, :], ACT.Ln, bias=K.c("eps")[:, 0:1], scale=1.0 / P).then_inc(*S(f"l{h}"))
                    act.wait_ge(*S.at(f"l{h}"))
                    act.activation(sq[:, h, :], sq[:, h, :], ACT.Exp, scale=-0.5).then_inc(*S(f"e{h}"))
                act.wait_ge(K.loaded, K.n_loaded)
                for h in hd:
                    act.activation(z[:, h, :], z[:, h, :], ACT.Silu).then_inc(*S(f"z{h}"))

            @block.vector
            def _(dve):
                dve.wait_ge(K.loaded, K.n_loaded)
                for h in hd:
                    dve.wait_ge(*S.at(f"e{h}"))
                    dve.scalar_tensor_tensor(OT[:, h, :], OT[:, h, :], nw[:, :], sq[:, h, :], ALU.mult,
                                             ALU.mult).then_inc(*V(f"n{h}"))
                    dve.wait_ge(*V.at(f"n{h}"))
                    dve.wait_ge(*S.at(f"z{h}"))
                    dve.tensor_tensor(OT[:, h, :], OT[:, h, :], z[:, h, :], ALU.mult).then_inc(*V(f"z{h}"))


def residual_take(K, H):
    def take(dve, u, bank, inc):
        c = u[0] * 512 + u[3]
        dst = H[:, u[2], c:c + 512]
        dve.scalar_tensor_tensor(dst, dst, ALPHA, bank, ALU.mult, ALU.add).then_inc(*inc)
    return take


def delta_net(K):
    nc = K.nc
    stage_to_cols(K, "x_cols", K.H, K.HT, NT)
    proj = nc.dram_tensor("proj_scratch", [32, P, T], F32, kind="Internal").ap()
    with nc.sbuf_tensor("gates", [P, 4, NT, HEADS], F32) as PH, nc.sbuf_tensor("chunk_decay", [P, HEADS, NCH], F32) as GL:
        stage_dn_projection(K, proj)
        stage_dn_gates(K, PH)
        with nc.sbuf_tensor("recurrence_in", [P, 3, HEADS, T], F32) as M3:
            M = [K.H[:, :, :].rearrange("p a (b n) -> p (a b) n", n=T), K.HT[:, :, :]] + [M3[:, i, :, :] for i in range(3)]
            stage_dn_heads(K, proj, PH, {"M": M, "GL": GL})
            stage_dn_recurrence(K, {"M": M, "GL": GL}, K.OT)
        stage_dn_output_norm(K, proj, K.OT)
    stage_gemm(K, "dn_out", [("rows", KD, 512)] * 2, K.OT, NT, None, residual_take(K, K.H))

def plan_experts(K, l):
    K.w.loads += [expert_load(K, l, q, part) for q, part in PAIR_PARTS]
    K.w.loads += [None] * (3 * (NE - 2))


PAIR_PARTS = [(0, 0), (0, 1), (1, 0), (1, 1), (0, 2), (1, 2)]


def expert_load(K, l, e, i):
    if i < 2:
        src = K.A["moe_w13"][l].rearrange("e (k p) n -> p e k n", p=P)[:, bass.ds(e, 1), :, 512 * i:512 * i + 512]
    else:
        src = K.A["moe_w2"][l].rearrange("e (k p) n -> p e k n", p=P)[:, bass.ds(e, 1), :, :]
    return src.rearrange("p e k n -> p (e k) n"), (8, 8, 4)[i], (512, 512, 1024)[i]


class Experts:

    POINTS = ["turned", "cols", "up", "silu", "hidden", "down", "y_act", "y_dve"]

    def __init__(self, K):
        nc = K.nc
        self.xs = nc.dram_tensor("block_rows_in", [ROWS + 2 * BLK, D], F32, kind="Internal").ap()
        self.ys = nc.dram_tensor("block_rows_out", [ROWS, D], F32, kind="Internal").ap()
        self.gates = nc.alloc_sbuf_tensor("pair_gates", [P, NT, 2], F32)
        self.rows = nc.alloc_sbuf_tensor("pair_rows", [P, NT, 2], I32)
        self.extra = nc.alloc_sbuf_tensor("extra_blocks", [P, EXTRA + 1], I32)
        self.cleared = nc.alloc_semaphore("block_rows_cleared")
        self.scattered = nc.alloc_semaphore("rows_scattered")
        self.gathered = [nc.alloc_semaphore(f"rows_gathered_{t}") for t in range(NT)]
        self.layers = 0

    def sems(self, nc, name):
        s = {x: nc.alloc_semaphore(f"{name}_{x}") for x in self.POINTS}
        s["x"] = nc.alloc_semaphore(f"{name}_x_landed")
        for q in range(2):
            s[f"y{q}"] = nc.alloc_semaphore(f"{name}_y_stored_{q}")
        return s


def stage_clear_block_rows(K, X):
    nc = K.nc
    zero = nc.alloc_semaphore("zero_rows")
    with nc.Block() as block:
        @block.vector
        def _(dve):
            dve.memset(K.OT[:, :, :], 0.0).then_inc(zero, 1)

        @block.scalar
        def _(act):
            act.wait_ge(zero, 1)
            for n in range(ROWS * D // (P * KD * T)):
                act.dma_start(X.xs[0:ROWS, :].rearrange("(a p b) d -> a p (b d)", p=P, b=4)[n],
                              K.OT[:, :, :].rearrange("p a b -> p (a b)")).then_inc(X.cleared, 16)
            act.dma_start(X.xs[ROWS:, :], K.OT[:, 0:D // T, :].rearrange("p a b -> p (a b)")).then_inc(X.cleared, 16)
            for n in range(NE * BLK // (4 * P), ROWS // (4 * P)):
                act.dma_start(X.ys.rearrange("(a p b) d -> a p (b d)", p=P, b=4)[n],
                              K.OT[:, :, :].rearrange("p a b -> p (a b)")).then_inc(X.cleared, 16)
            act.wait_ge(X.cleared, 16 * (ROWS + EXTRA * BLK) // (4 * P) + 16)


def stage_route(K, X, l, pre):
    nc, ps, A = K.nc, K.ps, K.A
    n = f"route{l}"
    with ExitStack() as mem:
        def sb(name, shape, dt=F32):
            return mem.enter_context(nc.sbuf_tensor(f"{n}_{name}", shape, dt))
        w = sb("w", [P, KD, NGRP + NE])
        lg = sb("lg", [P, NT, 8])
        el = sb("el", [P, NT, NE])
        gm = sb("gm", [P, NT, 8])
        gi = sb("gi", [P, NT, 8], U32)
        gf = sb("gf", [P, NT])
        mask = sb("mask", [P, NT, NE])
        low = sb("low", [P, NT, NE])
        v8 = sb("v8", [P, NT, 8])
        i8 = sb("i8", [P, NT, 8], U32)
        idx = sb("idx", [P, NT, 2])
        ex = sb("ex", [P, NT, NGRP])
        sm = sb("sm", [P, NT])
        dv = sb("dv", [P, NT])
        hot = sb("hot", [P, 2, NT, NE])
        both = sb("both", [P, NT, NE])
        cnt = sb("cnt", [P, NE])
        cmp_ = sb("cmp", [P, NE, 7])
        nx = sb("nx", [P, NE])
        one = sb("one", [P, NE])
        xe = sb("xe", [P, NE])
        delta = sb("delta", [P, NE])
        rank = sb("rank", [P, NT, NE])
        W = sb("W", [P, NT, NE])
        pick = sb("pick", [P, 2, NT, NE])
        dest = sb("dest", [P, NT, 2])
        ecmp = sb("ecmp", [P, EXTRA, NE])
        eb = sb("eb", [P, EXTRA + 1])
        tt = range(NT)
        E, S, V = K.steps("route", pe=["logits", "rank", "count"], act=["ex", "ed"],
                          dve=["pad", "lg", "el"] + [f"gm{t}" for t in tt] + [f"gi{t}" for t in tt] +
                          ["gf", "mask", "low", "el2", "el3"] + [f"v{t}" for t in tt] + [f"i{t}" for t in tt] +
                          ["idx", "hot0", "hot1", "both", "exd", "dv", "sm", "rs", "e1", "re", "g0", "g1",
                           "cnt", "cmp", "nx", "one", "xe", "delta", "delta2", "delta3", "rank", "ge", "gd", "W", "Wb",
                           "p0", "p1", "d0", "d1", "rows", "ecmp", "eb", "clip", "nxt", "ei"])
        logits = ps[0][:, 0:NT * (NGRP + NE)].rearrange("p (t c) -> p t c", t=NT)
        with nc.Block() as block:
            @block.sync
            def _(sp):
                K.load(sp, w[:, :, 0:NGRP], A["moe_w_group"][l].rearrange("(k p) n -> p k n", p=P))
                K.load(sp, w[:, :, NGRP:], A["moe_w_expert"][l].rearrange("(k p) n -> p k n", p=P))
                for sems in pre:
                    for x in X.POINTS:
                        sp.sem_inc(sems[x], 2)
                    for q in range(2):
                        sp.sem_inc(sems[f"y{q}"], 16)
                K.w.issue(sp, K.w.used + RING)

            @block.tensor
            def _(pe):
                pe.wait_ge(K.loaded, K.n_loaded)
                for t in tt:
                    for k in range(KD):
                        mm = pe.matmul(logits[:, t, :], K.HT[:, k, t * P:(t + 1) * P], w[:, k, :], start=k == 0,
                                       stop=k == KD - 1)
                mm.then_inc(*E("logits"))
                pe.wait_ge(*V.at("both"))
                for t in tt:
                    for u in range(t + 1):
                        mm = pe.matmul(ps[1][:, t * NE:(t + 1) * NE], K.c("before" if u == t else "ones"),
                                       both[:, u, :], start=u == 0, stop=u == t)
                mm.then_inc(*E("rank"))
                for u in tt:
                    mm = pe.matmul(ps[2][:, 0:NE], K.c("ones"), both[:, u, :], start=u == 0, stop=u == NT - 1)
                mm.then_inc(*E("count"))

            @block.scalar
            def _(act):
                act.wait_ge(*V.at("exd"))
                act.activation(ex[:, :, :], ex[:, :, :], ACT.Exp).then_inc(*S("ex"))
                act.wait_ge(*V.at("dv"))
                act.activation(dv[:, :], dv[:, :], ACT.Exp).then_inc(*S("ed"))

            @block.vector
            def _(dve):
                def at(label):
                    dve.wait_ge(*V.at(label))
                dve.memset(lg[:, :, :], NEG).then_inc(*V("pad"))
                dve.wait_ge(*E.at("logits"))
                at("pad")
                dve.tensor_copy(lg[:, :, 0:NGRP], logits[:, :, 0:NGRP]).then_inc(*V("lg"))
                dve.tensor_copy(el[:, :, :], logits[:, :, NGRP:]).then_inc(*V("el"))
                at("el")
                for t in tt:
                    dve.max(gm[:, t, :], lg[:, t, :]).then_inc(*V(f"gm{t}"))
                at(f"gm{NT - 1}")
                for t in tt:
                    dve.max_index(gi[:, t, :], gm[:, t, :], lg[:, t, :]).then_inc(*V(f"gi{t}"))
                at(f"gi{NT - 1}")
                dve.tensor_copy(gf[:, :], gi[:, :, 0]).then_inc(*V("gf"))
                at("gf")
                dve.tensor_tensor(mask[:, :, :], bm(K.c("group32"), NT), bc(gf[:, :], NE), ALU.is_equal).then_inc(*V("mask"))
                at("mask")
                dve.tensor_scalar(low[:, :, :], mask[:, :, :], -NEG, NEG, ALU.mult, ALU.add).then_inc(*V("low"))
                dve.tensor_tensor(el[:, :, :], el[:, :, :], mask[:, :, :], ALU.mult).then_inc(*V("el2"))
                at("el2")
                dve.tensor_tensor(el[:, :, :], el[:, :, :], low[:, :, :], ALU.add).then_inc(*V("el3"))
                at("el3")
                for t in tt:
                    dve.max(v8[:, t, :], el[:, t, :]).then_inc(*V(f"v{t}"))
                at(f"v{NT - 1}")
                for t in tt:
                    dve.max_index(i8[:, t, :], v8[:, t, :], el[:, t, :]).then_inc(*V(f"i{t}"))
                at(f"i{NT - 1}")
                dve.tensor_copy(idx[:, :, :], i8[:, :, 0:2]).then_inc(*V("idx"))
                at("idx")
                for j in range(2):
                    dve.tensor_tensor(hot[:, j, :, :], bm(K.c("iota32"), NT), bc(idx[:, :, j], NE),
                                      ALU.is_equal).then_inc(*V(f"hot{j}"))
                at("hot1")
                dve.tensor_tensor(both[:, :, :], hot[:, 0, :, :], hot[:, 1, :, :], ALU.add).then_inc(*V("both"))
                dve.tensor_tensor(ex[:, :, :], lg[:, :, 0:NGRP], bc(gm[:, :, 0], NGRP), ALU.subtract).then_inc(*V("exd"))
                dve.tensor_tensor(dv[:, :], v8[:, :, 1], v8[:, :, 0], ALU.subtract).then_inc(*V("dv"))
                dve.wait_ge(*S.at("ex"))
                dve.reduce_sum(sm[:, :], ex[:, :, :], AX.X).then_inc(*V("sm"))
                at("sm")
                dve.reciprocal(sm[:, :], sm[:, :]).then_inc(*V("rs"))
                dve.wait_ge(*S.at("ed"))
                dve.tensor_scalar(gf[:, :], dv[:, :], 1.0, None, ALU.add).then_inc(*V("e1"))
                at("e1")
                dve.reciprocal(gf[:, :], gf[:, :]).then_inc(*V("re"))
                at("re")
                dve.tensor_tensor(X.gates[:, :, 0], gf[:, :], sm[:, :], ALU.mult).then_inc(*V("g0"))
                at("g0")
                dve.tensor_tensor(X.gates[:, :, 1], X.gates[:, :, 0], dv[:, :], ALU.mult).then_inc(*V("g1"))
                dve.wait_ge(*E.at("count"))
                dve.tensor_copy(cnt[:, :], ps[2][:, 0:NE]).then_inc(*V("cnt"))
                at("cnt")
                dve.tensor_tensor(cmp_[:, :, :], bc(cnt[:, :], 7), bm(K.c("multiple8")[:, 1:8], NE), ALU.is_gt).then_inc(*V("cmp"))
                at("cmp")
                dve.reduce_sum(nx[:, :], cmp_[:, :, :], AX.X).then_inc(*V("nx"))
                dve.memset(one[:, :], 1.0).then_inc(*V("one"))
                at("one")
                dve.tensor_tensor_scan(xe[:, :], one[:, :], nx[:, :], 0.0, ALU.mult, ALU.add).then_inc(*V("xe"))
                at("xe")
                dve.tensor_tensor(delta[:, :], xe[:, :], nx[:, :], ALU.subtract).then_inc(*V("delta"))
                at("delta")
                dve.tensor_scalar(delta[:, :], delta[:, :], float(BLK), float((NE - 1) * BLK), ALU.mult, ALU.add).then_inc(*V("delta2"))
                at("delta2")
                dve.tensor_tensor(delta[:, :], delta[:, :], K.c("base32"), ALU.subtract).then_inc(*V("delta3"))
                dve.wait_ge(*E.at("rank"))
                dve.tensor_copy(rank[:, :, :], ps[1][:, 0:NT * NE].rearrange("p (t e) -> p t e", t=NT)).then_inc(*V("rank"))
                at("rank")
                dve.tensor_scalar(W[:, :, :], rank[:, :, :], float(BLK), None, ALU.is_ge).then_inc(*V("ge"))
                at("ge")
                dve.tensor_tensor(W[:, :, :], W[:, :, :], bm(delta[:, :], NT), ALU.mult).then_inc(*V("gd"))
                at("gd")
                dve.tensor_tensor(W[:, :, :], W[:, :, :], rank[:, :, :], ALU.add).then_inc(*V("W"))
                at("W")
                dve.tensor_tensor(W[:, :, :], W[:, :, :], bm(K.c("base32"), NT), ALU.add).then_inc(*V("Wb"))
                at("Wb")
                for j in range(2):
                    dve.tensor_tensor(pick[:, j, :, :], W[:, :, :], hot[:, j, :, :], ALU.mult).then_inc(*V(f"p{j}"))
                at("p1")
                for j in range(2):
                    dve.reduce_sum(dest[:, :, j], pick[:, j, :, :], AX.X).then_inc(*V(f"d{j}"))
                at("d1")
                dve.tensor_copy(X.rows[:, :, :], dest[:, :, :]).then_inc(*V("rows"))
                dve.tensor_tensor(ecmp[:, :, :], bm(xe[:, :], EXTRA), bc(K.c("iota16"), NE), ALU.is_le).then_inc(*V("ecmp"))
                at("ecmp")
                dve.reduce_sum(eb[:, 0:EXTRA], ecmp[:, :, :], AX.X).then_inc(*V("eb"))
                at("eb")
                dve.tensor_scalar(eb[:, 0:EXTRA], eb[:, 0:EXTRA], float(NE - 1), None, ALU.min).then_inc(*V("clip"))
                dve.tensor_copy(eb[:, EXTRA:], xe[:, NE - 1:]).then_inc(*V("nxt"))
                at("nxt")
                dve.tensor_copy(X.extra[:, :], eb[:, :]).then_inc(*V("ei"))

            @block.gpsimd
            def _(pool):
                pool.wait_ge(*V.at("rows"))
                for t in tt:
                    for j in range(2):
                        pool.indirect_dma_start(X.xs, bass.IndirectOffsetOnAxis(ap=X.rows[:, t, j:j + 1].bitcast(U32), axis=0),
                                                K.H[:, t, :], None).then_inc(X.scattered, 16)
                pool.wait_ge(X.scattered, 16 * 2 * NT * X.layers)


class BlockPair:

    def __init__(self, K, X, sems, mem, name):
        nc = K.nc
        self.K, self.X, self.s = K, X, sems

        def sb(n, shape):
            return [mem.enter_context(nc.sbuf_tensor(f"{name}_{n}{q}", shape, F32)) for q in range(2)]
        self.xin = mem.enter_context(nc.sbuf_tensor(f"{name}_xin", [2 * BLK, D], F32))
        self.xT = mem.enter_context(nc.sbuf_tensor(f"{name}_xT", [P, KD, 2 * BLK], F32))
        self.sg = sb("sg", [P, 4, BLK])
        self.hid = sb("hid", [P, 4, BLK])
        self.y = sb("y", [BLK, D])

    def passed(self, x, b):
        return self.s[x], b + 3

    def freed(self, x, b):
        return self.s[x], b + 1

    def load_x(self, eng, j):
        eng.dma_start(self.xin[:, :], self.X.xs[bass.ds(2 * BLK * j, 2 * BLK), :]).then_inc(self.s["x"], 16)

    def turn(self, pe, j):
        ps = self.K.ps
        pe.wait_ge(self.s["x"], 16 * j + 16)
        for half in range(2):
            for k in range(4):
                mm = pe.transpose(ps[half][:, k * P:(k + 1) * P],
                                  self.xin[:, (4 * half + k) * P:(4 * half + k + 1) * P], self.K.c("ident"))
            mm.then_inc(self.s["turned"], 1)

    def take_cols(self, act, j):
        act.wait_ge(*self.freed("up", 2 * j + 1))
        for half in range(2):
            act.wait_ge(*self.passed("turned", 2 * j + half))
            act.activation(self.xT[:, 4 * half:4 * half + 4, :],
                           self.K.ps[half][:, :].rearrange("p (k n) -> p k n", k=4), ACT.Copy).then_inc(self.s["cols"], 1)

    def tensor(self, pe, j, landed, slots):
        ps = self.K.ps
        pe.wait_ge(*self.passed("cols", 2 * j + 1))
        for q in range(2):
            b = 2 * j + q
            pe.wait_ge(*self.freed("hidden", b))
            for part in range(2):
                landed(pe, q, part)
                w = slots(q, part)
                for f in range(4):
                    for k in range(KD):
                        mm = pe.matmul(ps[2 + q][:, (part * 4 + f) * BLK:(part * 4 + f + 1) * BLK],
                                       w[:, k, f * P:(f + 1) * P], self.xT[:, k, q * BLK:(q + 1) * BLK],
                                       start=k == 0, stop=k == KD - 1)
            mm.then_inc(self.s["up"], 1)
        self.turn(pe, j + 1)
        for q in range(2):
            b = 2 * j + q
            pe.wait_ge(*self.passed("hidden", b))
            landed(pe, q, 2)
            pe.wait_ge(*self.freed("y_act", b))
            pe.wait_ge(*self.freed("y_dve", b))
            w = slots(q, 2)
            for c in range(2):
                for f in range(4):
                    mm = pe.matmul(ps[4 + 2 * q + c][0:BLK, :], self.hid[q][:, f, :], w[:, f, c * 512:c * 512 + 512],
                                   start=f == 0, stop=f == 3)
            mm.then_inc(self.s["down"], 1)

    def scalar(self, act, j):
        ps = self.K.ps
        self.load_x(act, j + 1)
        for q in range(2):
            b = 2 * j + q
            act.wait_ge(*self.passed("up", b))
            act.wait_ge(*self.freed("hidden", b))
            act.activation(self.sg[q][:, :, :], ps[2 + q][:, 0:4 * BLK].rearrange("p (k n) -> p k n", k=4),
                           ACT.Silu).then_inc(self.s["silu"], 1)
        self.take_cols(act, j + 1)
        for q in range(2):
            b = 2 * j + q
            act.wait_ge(*self.passed("down", b))
            act.wait_ge(self.s[f"y{q}"], 16 * j + 16)
            act.activation(self.y[q][:, 0:512], ps[4 + 2 * q][0:BLK, :], ACT.Copy).then_inc(self.s["y_act"], 1)
            act.wait_ge(*self.passed("y_act", b))
            act.wait_ge(*self.passed("y_dve", b))
            act.dma_start(self.X.ys[bass.ds(b * BLK, BLK), :], self.y[q][:, :]).then_inc(self.s[f"y{q}"], 16)

    def vector(self, dve, j):
        ps = self.K.ps
        for q in range(2):
            b = 2 * j + q
            dve.wait_ge(*self.passed("silu", b))
            dve.wait_ge(*self.freed("down", b))
            dve.tensor_tensor(self.hid[q][:, :, :], ps[2 + q][:, 4 * BLK:8 * BLK].rearrange("p (k n) -> p k n", k=4),
                              self.sg[q][:, :, :], ALU.mult).then_inc(self.s["hidden"], 1)
        for q in range(2):
            b = 2 * j + q
            dve.wait_ge(*self.passed("down", b))
            dve.wait_ge(self.s[f"y{q}"], 16 * j + 16)
            dve.tensor_copy(self.y[q][:, 512:1024], ps[5 + 2 * q][0:BLK, :]).then_inc(self.s["y_dve"], 1)


def stage_experts(K, X, l, sems):
    nc = K.nc
    n0 = K.w.used
    main, last = NE // 2, (NE + EXTRA) // 2
    extra_landed = [nc.alloc_semaphore(f"experts{l}_extra_landed_{i}") for i in range(6)]
    assert K.w.issued == n0 + RING, "the first pair's weights are on their way"
    K.w.issued = n0 + 3 * NE
    K.w.used = n0 + 3 * NE
    with ExitStack() as mem:
        B = BlockPair(K, X, sems, mem, f"experts{l}")

        def slots(q, part):
            k, w = ((KD, 512), (KD, 512), (4, 1024))[part]
            return K.w.slot(n0 + PAIR_PARTS.index((q, part)), k, w)

        for i, (q, part) in enumerate(PAIR_PARTS):
            K.w.free[n0 + 3 * NE - RING + i] = B.passed("down" if part == 2 else "up", NE - 2 + q)

        def has_rows(j, n):
            return 2 * j < n

        def blocks(eng):
            return eng.value_load(X.extra[0:1, EXTRA:EXTRA + 1], min_val=0, max_val=EXTRA - 1) + NE

        def load(sp, j, q, part, e, landed):
            sp.wait_ge(*B.freed("down" if part == 2 else "up", 2 * j + q))
            src, k, w = expert_load(K, l, e, part)
            sp.dma_start(slots(q, part), src).then_inc(landed, 16)

        with nc.Block() as block:
            @block.sync
            def _(sp):
                with sp.Fori(1, main) as j:
                    for i, (q, part) in enumerate(PAIR_PARTS):
                        load(sp, j, q, part, 2 * j + q, K.w.landed[(n0 + i) % RING])
                n = blocks(sp)
                with sp.Fori(main, last) as j:
                    with sp.If(has_rows(j, n)):
                        e = [sp.value_load(X.extra[0:1, bass.ds(2 * j + q - NE, 1)], min_val=0, max_val=NE - 1)
                             for q in range(2)]
                        for i, (q, part) in enumerate(PAIR_PARTS):
                            load(sp, j, q, part, e[q], extra_landed[i])

            @block.tensor
            def _(pe):
                B.turn(pe, 0)
                with pe.Fori(0, main) as j:
                    def landed(pe, q, part):
                        n = n0 + PAIR_PARTS.index((q, part))
                        pe.wait_ge(K.w.landed[n % RING], 16 * (n // RING + 1) + 16 * j)
                    B.tensor(pe, j, landed, slots)
                n = blocks(pe)
                with pe.Fori(main, last) as j:
                    def landed(pe, q, part):
                        pe.wait_ge(extra_landed[PAIR_PARTS.index((q, part))], 16 * j + 16 - 16 * main)
                    with pe.If(has_rows(j, n)):
                        B.tensor(pe, j, landed, slots)

            @block.scalar
            def _(act):
                B.load_x(act, 0)
                B.take_cols(act, 0)
                with act.Fori(0, main) as j:
                    B.scalar(act, j)
                n = blocks(act)
                with act.Fori(main, last) as j:
                    with act.If(has_rows(j, n)):
                        B.scalar(act, j)

            @block.vector
            def _(dve):
                with dve.Fori(0, main) as j:
                    B.vector(dve, j)
                n = blocks(dve)
                with dve.Fori(main, last) as j:
                    with dve.If(has_rows(j, n)):
                        B.vector(dve, j)

            @block.gpsimd
            def _(pool):
                for q in range(2):
                    pool.wait_ge(sems[f"y{q}"], 16 * main + 16)
                n = blocks(pool)
                with pool.Fori(main, last) as j:
                    with pool.If(has_rows(j, n)):
                        for q in range(2):
                            pool.wait_ge(sems[f"y{q}"], 16 * j + 32)


def stage_combine(K, X, l):
    nc = K.nc
    with nc.sbuf_tensor(f"picked{l}", [P, NT, D], F32) as Y1:
        Y0 = K.OT[:, :, :].rearrange("p (t a) n -> p t (a n)", t=NT)
        V, = K.steps("combine", dve=[f"{x}{t}" for t in range(NT) for x in ("a", "b", "c")])
        with nc.Block() as block:
            @block.sync
            def _(sp):
                K.w.issue(sp, K.w.used + RING)

            @block.gpsimd
            def _(pool):
                for t in range(NT):
                    for j, Y in enumerate((Y0, Y1)):
                        pool.indirect_dma_start(Y[:, t, :], None, X.ys,
                                                bass.IndirectOffsetOnAxis(ap=X.rows[:, t, j:j + 1].bitcast(U32), axis=0)
                                                ).then_inc(X.gathered[t], 16)

            @block.vector
            def _(dve):
                for t in range(NT):
                    dve.tensor_scalar(K.H[:, t, :], K.H[:, t, :], ALPHA, None, ALU.mult).then_inc(*V(f"a{t}"))
                    dve.wait_ge(*V.at(f"a{t}"))
                    dve.wait_ge(X.gathered[t], 32 * X.layers)
                    dve.scalar_tensor_tensor(K.H[:, t, :], Y0[:, t, :], X.gates[:, t, 0:1], K.H[:, t, :], ALU.mult,
                                             ALU.add).then_inc(*V(f"b{t}"))
                    dve.wait_ge(*V.at(f"b{t}"))
                    dve.scalar_tensor_tensor(K.H[:, t, :], Y1[:, t, :], X.gates[:, t, 1:2], K.H[:, t, :], ALU.mult,
                                             ALU.add).then_inc(*V(f"c{t}"))


def moe_layer(K, X, l):
    nc = K.nc
    X.layers += 1
    sems = X.sems(nc, f"experts{l}")
    stage_to_cols(K, f"ffn_cols{l}", K.H, K.HT, NT)
    stage_route(K, X, l, [sems])
    stage_experts(K, X, l, sems)
    stage_combine(K, X, l)
    stage_layer_norm(K, f"ln_ffn{l}", K.H, K.A["ln_ffn_g"][l], K.A["ln_ffn_b"][l])

def stage_attention(K, name, mode, Q, KT, V, out, chunks, tiles, nkeys, rpb=None, lam=None):
    nc = K.nc
    diff, pairs = mode == "diff", mode == "pairs"
    heads = 1 if diff else 2
    hw = 128 if diff else 64
    units = [(hh, t) for hh in range(heads) for t in range(tiles)]
    nu = len(units)
    nq = tiles * P

    def width(u):
        return (units[u][1] + 1) * P if diff else nkeys

    pool_labels = ["q"] + (["k"] if mode != "shared" else []) + (["b0", "b1"] if rpb is not None else [])
    dve_labels = []

    def dve_first(u):
        return ([f"c0{u}", f"c1{u}"] if diff else [f"c0{u}"] if rpb is not None else []) + [f"m{u}"]
    for u in range(min(2, nu)):
        dve_labels += dve_first(u)
    for u in range(nu):
        dve_labels += ([f"r{u}", f"r1{u}", f"a{u}", f"b{u}"] if diff else [f"r{u}"]) + [f"tv{u}"]
        if u + 2 < nu:
            dve_labels += dve_first(u + 2)
        dve_labels += [f"o{u}"]
    pe_labels = [f"S{u}" for u in range(min(2, nu))]
    act_labels = [f"e{u}" for u in range(min(2, nu))]
    for u in range(nu):
        pe_labels += [f"T{u}"] + ([f"S{u + 2}"] if u + 2 < nu else []) + [f"V{u}"]
        act_labels += [f"ta{u}"] + ([f"e{u + 2}"] if u + 2 < nu else [])
    E, S, D_, G = K.steps("attention", turns=chunks, pe=pe_labels, act=act_labels, dve=dve_labels, pool=pool_labels)
    biased = nc.alloc_semaphore(f"{name}_bias_landed") if rpb is not None else None
    last = units.index(units[-1])
    with ExitStack() as mem:
        def sb(n, shape):
            return mem.enter_context(nc.sbuf_tensor(f"{name}_{n}", shape, F32))
        qs = sb("q", [P, nq])
        ks = sb("k", [P, nkeys]) if mode != "shared" else None
        pm = sb("p", [P, 2, 1024 if diff else nkeys])
        pT = sb("pT", [P, 2, 512 if diff else nkeys])
        sm = sb("sum", [P, 4, 2])
        mx = sb("max", [P, 2, 2])
        if rpb is not None:
            bias = sb("bias", [P, 2, 16, 64])

        def scores(u):
            b = K.bank[:, 2 * (u % 2):2 * (u % 2) + 2, :]
            return b[:, :, 0:width(u)] if diff else b.rearrange("p a n -> p (a n)")[:, 0:nkeys]

        def probs(u):
            p = pm[:, u % 2, :]
            return p.rearrange("p (a n) -> p a n", a=2)[:, :, 0:width(u)] if diff else p

        def summed(u):
            return probs(u)[:, 0, :] if diff else probs(u)

        def halves(u):
            n = width(u)
            return (slice(0, min(n, 384)), slice(min(n, 384), n)) if n > 384 else (slice(0, n // 2), slice(n // 2, n))

        def turned(u):
            return K.bank[:, 4:6, :].rearrange("p a n -> p (a n)")[:, 0:width(u)]

        with nc.Block() as block:
            @block.sync
            def _(sp):
                if rpb is not None:
                    with sp.Fori(0, chunks) as c:
                        sp.wait_ge(*G.before(c))
                        sp.wait_ge(*D_.before(c))
                        for hh in range(2):
                            for half in range(2):
                                src = rpb[bass.ds(2 * c + hh, 1), :, :, :].rearrange("a q i n -> (a q) i n")
                                sp.dma_start(bias[64 * half:64 * half + 64, hh, half:15 + half, :], src).then_inc(biased, 16)
                K.w.issue(sp, K.w.used + K.w.ring)

            @block.gpsimd
            def _(pool):
                with pool.Fori(0, chunks) as c:
                    pool.wait_ge(*E.before(c))
                    pool.tensor_copy(qs[:, :], Q[:, bass.ds(c, 1), 0:nq].rearrange("p a n -> p (a n)")).then_inc(*G("q"))
                    if mode != "shared":
                        pool.tensor_copy(ks[:, :], KT[:, bass.ds(c, 1), 0:nkeys].rearrange("p a n -> p (a n)")).then_inc(*G("k"))
                    if rpb is not None:
                        pool.wait_ge(biased, 64 * c + 64)
                        for hh in range(2):
                            v = bias[:, hh, 1:15, :]
                            pool.tensor_tensor(v, v, bm(K.c("win_neg"), 14), ALU.add).then_inc(*G(f"b{hh}"))

            @block.tensor
            def _(pe):
                with pe.Fori(0, chunks) as c:
                    def score(u):
                        hh, t = units[u]
                        if u < 2:
                            pe.wait_ge(*G.at("q" if mode == "shared" else "k", c))
                        else:
                            pe.wait_ge(*S.at(f"e{u - 2}", c))
                        b = 2 * (u % 2)
                        if diff:
                            for s in range(2):
                                r = slice(64 * s, 64 * s + 64)
                                mm = pe.matmul(K.bank[:, b + s, 0:width(u)], qs[r, t * P:(t + 1) * P], ks[r, 0:width(u)],
                                               start=True, stop=True)
                        else:
                            r = slice(64 * hh, 64 * hh + 64)
                            src = ks[r, :] if mode != "shared" else KT[r, 0, 0:nkeys]
                            for i, a in enumerate(range(0, nkeys, 512)):
                                n = min(512, nkeys - a)
                                mm = pe.matmul(K.bank[:, b + i, 0:n], qs[r, t * P:(t + 1) * P], src[:, a:a + n],
                                               start=True, stop=True)
                        mm.then_inc(*E(f"S{u}"))

                    def turn(u):
                        pe.wait_ge(*(D_.at(f"b{u}", c) if diff else S.at(f"e{u}", c)))
                        if u >= 1:
                            pe.wait_ge(*S.at(f"ta{u - 1}", c))
                            pe.wait_ge(*D_.at(f"tv{u - 1}", c))
                        for i in range(width(u) // P):
                            mm = pe.transpose(turned(u)[:, i * P:(i + 1) * P], summed(u)[:, i * P:(i + 1) * P], K.c("ident"))
                        mm.then_inc(*E(f"T{u}"))

                    def values(u):
                        hh, t = units[u]
                        pe.wait_ge(*S.at(f"ta{u}", c))
                        pe.wait_ge(*D_.at(f"tv{u}", c))
                        if u >= 2:
                            pe.wait_ge(*D_.at(f"o{u - 2}", c))
                        n = width(u) // P
                        for i in range(n):
                            if mode == "shared":
                                v = V[:, i, hh * 64:hh * 64 + 64]
                            else:
                                v = V[:, i, bass.ds(c * P + hh * 64, hw)]
                            mm = pe.matmul(K.bank[:, 6 + u % 2, 0:hw], pT[:, u % 2, i * P:(i + 1) * P], v, start=i == 0,
                                           stop=i == n - 1)
                        mm.then_inc(*E(f"V{u}"))

                    for u in range(min(2, nu)):
                        score(u)
                    for u in range(nu):
                        turn(u)
                        if u + 2 < nu:
                            score(u + 2)
                        values(u)

            @block.scalar
            def _(act):
                with act.Fori(0, chunks) as c:
                    def exps(u):
                        act.wait_ge(*D_.at(f"m{u}", c))
                        if u >= 2:
                            act.wait_ge(*E.at(f"T{u - 2}", c))
                        if u >= 4:
                            act.wait_ge(*D_.at(f"o{u - 4}", c))
                        if diff:
                            for s in range(2):
                                i = act.activation(probs(u)[:, s, :], scores(u)[:, s, :], ACT.Exp, bias=mx[:, u % 2, s:s + 1],
                                                   accum_out=sm[:, u % 4, s:s + 1])
                            i.then_inc(*S(f"e{u}"))
                        else:
                            act.activation(probs(u), scores(u), ACT.Exp, bias=mx[:, u % 2, 0:1],
                                           accum_out=sm[:, u % 4, 0:1]).then_inc(*S(f"e{u}"))
                    for u in range(min(2, nu)):
                        exps(u)
                    for u in range(nu):
                        act.wait_ge(*E.at(f"T{u}", c))
                        if u >= 2:
                            act.wait_ge(*E.at(f"V{u - 2}", c))
                        h = halves(u)[0]
                        act.activation(pT[:, u % 2, h], turned(u)[:, h], ACT.Copy).then_inc(*S(f"ta{u}"))
                        if u + 2 < nu:
                            exps(u + 2)

            @block.vector
            def _(dve):
                with dve.Fori(0, chunks) as c:
                    def first(u):
                        hh, t = units[u]
                        dve.wait_ge(*E.at(f"S{u}", c))
                        if diff:
                            for s in range(2):
                                d = scores(u)[:, s, t * P:(t + 1) * P]
                                dve.tensor_tensor(d, d, K.c("tril_neg"), ALU.add).then_inc(*D_(f"c{s}{u}"))
                            dve.wait_ge(*D_.at(f"c1{u}", c))
                        elif rpb is not None:
                            if u == 0:
                                dve.wait_ge(*G.at("b1", c))
                            d = scores(u)[:, 0:512]
                            dve.tensor_tensor(d, d, bias[:, hh, 7 - 2 * t:15 - 2 * t, :].rearrange("p a n -> p (a n)"),
                                              ALU.add).then_inc(*D_(f"c0{u}"))
                            dve.wait_ge(*D_.at(f"c0{u}", c))
                        if u >= 2:
                            dve.wait_ge(*S.at(f"e{u - 2}", c))
                        n = 2 if diff else 1
                        dve.reduce_max(mx[:, u % 2, 0:n], scores(u), AX.X, negate=True).then_inc(*D_(f"m{u}"))

                    for u in range(min(2, nu)):
                        first(u)
                    for u in range(nu):
                        hh, t = units[u]
                        dve.wait_ge(*S.at(f"e{u}", c))
                        n = 2 if diff else 1
                        dve.reciprocal(sm[:, u % 4, 0:n], sm[:, u % 4, 0:n]).then_inc(*D_(f"r{u}"))
                        if diff:
                            dve.wait_ge(*D_.at(f"r{u}", c))
                            dve.tensor_tensor(sm[:, u % 4, 1:2], sm[:, u % 4, 1:2], lam[:, 0:1], ALU.mult).then_inc(*D_(f"r1{u}"))
                            dve.wait_ge(*D_.at(f"r1{u}", c))
                            dve.tensor_scalar(probs(u)[:, 1, :], probs(u)[:, 1, :], sm[:, u % 4, 1:2], None,
                                              ALU.mult).then_inc(*D_(f"a{u}"))
                            dve.wait_ge(*D_.at(f"a{u}", c))
                            dve.scalar_tensor_tensor(probs(u)[:, 0, :], probs(u)[:, 0, :], sm[:, u % 4, 0:1], probs(u)[:, 1, :],
                                                     ALU.mult, ALU.subtract).then_inc(*D_(f"b{u}"))
                        dve.wait_ge(*E.at(f"T{u}", c))
                        dve.wait_ge(*S.at(f"ta{u}", c))
                        h = halves(u)[1]
                        dve.tensor_copy(pT[:, u % 2, h], turned(u)[:, h]).then_inc(*D_(f"tv{u}"))
                        if u + 2 < nu:
                            first(u + 2)
                        dve.wait_ge(*E.at(f"V{u}", c))
                        if mode == "shared":
                            dst = out[:, t, bass.ds(hh * 256 + c * 64, 64)]
                        else:
                            dst = out[:, t, bass.ds(c * P + hh * 64, hw)]
                        if diff:
                            dve.tensor_copy(dst, K.bank[:, 6 + u % 2, 0:hw]).then_inc(*D_(f"o{u}"))
                        else:
                            dve.wait_ge(*D_.at(f"r{u}", c))
                            dve.tensor_scalar(dst, K.bank[:, 6 + u % 2, 0:hw], sm[:, u % 4, 0:1], None,
                                              ALU.mult).then_inc(*D_(f"o{u}"))



def plan_differential(K):
    for g in range(4):
        plan_gemm(K, K.A["kv_w"], 512 * g, 512, KD)
    for g in range(2):
        plan_gemm(K, K.A["b_w_q"][0], 512 * g, 512, KD)
    for g in range(2):
        plan_gemm(K, K.A["b_w_out"][0], 512 * g, 512, KD)


def stage_lambda(K, lam, par, prod):
    nc = K.nc
    S, V = K.steps("lambda", act=["e"], dve=["p", "s", "d", "lam"])
    with nc.Block() as block:
        @block.sync
        def _(sp):
            K.load(sp, par[:, :, :], K.A["b_lambda"][0].rearrange("a n -> (a n)").partition_broadcast(P)
                   .rearrange("p (a n) -> p a n", a=4))
            K.w.issue(sp, K.w.used + K.w.ring)

        @block.vector
        def _(dve):
            dve.wait_ge(K.loaded, K.n_loaded)
            v = par[:, :, :].rearrange("p (a b) n -> p a b n", b=2)
            dve.tensor_tensor(prod[:, :, :], v[:, :, 0, :], v[:, :, 1, :], ALU.mult).then_inc(*V("p"))
            dve.wait_ge(*V.at("p"))
            dve.reduce_sum(lam[:, 0:2], prod[:, :, :], AX.X).then_inc(*V("s"))
            dve.wait_ge(*S.at("e"))
            dve.tensor_tensor(lam[:, 0:1], lam[:, 0:1], lam[:, 1:2], ALU.subtract).then_inc(*V("d"))
            dve.wait_ge(*V.at("d"))
            dve.tensor_scalar(lam[:, 0:1], lam[:, 0:1], LAMBDA_INIT, None, ALU.add).then_inc(*V("lam"))

        @block.scalar
        def _(act):
            act.wait_ge(*V.at("s"))
            act.activation(lam[:, 0:2], lam[:, 0:2], ACT.Exp).then_inc(*S("e"))


def stage_sub_norm(K, O):
    nc = K.nc
    with ExitStack() as mem:
        sq = mem.enter_context(nc.sbuf_tensor("sub_sq", [P, NT, D], F32))
        ss = mem.enter_context(nc.sbuf_tensor("sub_ss", [P, NT, HEADS], F32))
        w = mem.enter_context(nc.sbuf_tensor("sub_w", [P, P], F32))
        tt = range(NT)
        S, V = K.steps("sub_norm", act=[f"q{t}" for t in tt] + ["ln", "rs"],
                       dve=["w"] + [f"s{t}" for t in tt] + [f"{x}{t}" for t in tt for x in ("n", "g")])

        def heads(x, t):
            return x[:, t, :].rearrange("p (h n) -> p h n", h=HEADS)
        with nc.Block() as block:
            @block.sync
            def _(sp):
                K.load(sp, w[:, :], K.A["b_subln_w"][0].partition_broadcast(P))
                K.w.issue(sp, K.w.used + K.w.ring)

            @block.scalar
            def _(act):
                for t in tt:
                    act.activation(sq[:, t, :], O[:, t, :], ACT.Square).then_inc(*S(f"q{t}"))
                act.wait_ge(*V.at(f"s{NT - 1}"))
                act.activation(ss[:, :, :], ss[:, :, :], ACT.Ln, scale=1.0 / P, bias=K.c("eps")[:, 0:1]).then_inc(*S("ln"))
                act.wait_ge(*S.at("ln"))
                act.activation(ss[:, :, :], ss[:, :, :], ACT.Exp, scale=-0.5).then_inc(*S("rs"))

            @block.vector
            def _(dve):
                dve.wait_ge(K.loaded, K.n_loaded)
                dve.tensor_scalar(w[:, :], w[:, :], 1.0 - LAMBDA_INIT, None, ALU.mult).then_inc(*V("w"))
                for t in tt:
                    dve.wait_ge(*S.at(f"q{t}"))
                    dve.reduce_sum(ss[:, t, :], heads(sq, t), AX.X).then_inc(*V(f"s{t}"))
                dve.wait_ge(*S.at("rs"))
                for t in tt:
                    dve.tensor_tensor(heads(O, t), heads(O, t), bc(ss[:, t, :], P), ALU.mult).then_inc(*V(f"n{t}"))
                    dve.wait_ge(*V.at(f"n{t}"))
                    dve.tensor_tensor(heads(O, t), heads(O, t), bm(w[:, :], HEADS), ALU.mult).then_inc(*V(f"g{t}"))


def copy_take(dst, scale=1.0):
    def act(e, u, bank, inc):
        e.activation(dst(u), bank, ACT.Copy, scale=scale).then_inc(*inc)

    def dve(e, u, bank, inc):
        if scale == 1.0:
            e.tensor_copy(dst(u), bank).then_inc(*inc)
        else:
            e.tensor_scalar(dst(u), bank, scale, None, ALU.mult).then_inc(*inc)
    return act, dve


def differential(K):
    nc = K.nc
    stage_to_cols(K, "diff_cols", K.H, K.HT, NT)
    with ExitStack() as mem:
        lam = mem.enter_context(nc.sbuf_tensor("lam", [P, 2], F32))
        with nc.sbuf_tensor("lam_par", [P, 4, 64], F32) as par, nc.sbuf_tensor("lam_prod", [P, 2, 64], F32) as prod:
            stage_lambda(K, lam, par, prod)
        with ExitStack() as kv:
            KT = kv.enter_context(nc.sbuf_tensor("diff_keys", [P, KD, T], F32))
            V = kv.enter_context(nc.sbuf_tensor("diff_vals", [P, NT, D], F32))
            stage_gemm(K, "diff_k", [("cols", KD, 512)] * 2, K.HT, NT, *copy_take(lambda u: KT[:, 4 * u[0] + u[2], :]))
            stage_gemm(K, "diff_v", [("rows", KD, 512)] * 2, K.HT, NT,
                       *copy_take(lambda u: V[:, u[2], 512 * u[0]:512 * u[0] + 512]))
            stage_gemm(K, "diff_q", [("cols", KD, 512)] * 2, K.HT, NT,
                       *copy_take(lambda u: K.OT[:, 4 * u[0] + u[2], :], 0.125))
            O = K.HT[:, :, :].rearrange("p (t a) n -> p t (a n)", t=NT)
            stage_attention(K, "diff", "diff", K.OT, KT, V, O, HEADS, NT, T, lam=lam)
        stage_sub_norm(K, O)
    stage_to_cols(K, "diff_out_cols", O, K.OT, NT)
    stage_gemm(K, "diff_out", [("rows", KD, 512)] * 2, K.OT, NT, None, residual_take(K, K.H))

RING2 = 3
NA_W = 512
TA = T + CTX
RPB_R, RPB_C = 15, 31


def rope_tables():
    d = np.arange(P) % 64
    inv = (1.0 / (np.float32(10000.0) ** (np.arange(16, dtype=np.float32) / np.float32(16)))).astype(np.float32)
    t = np.arange(T)
    pos = np.where((d // 32 == 0)[:, None], (t // 64)[None, :], (t % 64)[None, :]).astype(np.float32)
    ang = (pos * inv[d % 16][:, None]).astype(np.float32)
    sign = np.where((d % 32) // 16 == 0, -1.0, 1.0).astype(np.float32)[:, None]
    return np.concatenate([np.cos(ang), np.sin(ang) * sign], axis=1).astype(np.float32)


class Unit:

    def __init__(self, g, kd, width, lhs, rhs, shape, on, take):
        self.g, self.kd, self.width, self.lhs, self.rhs = g, kd, width, lhs, rhs
        self.shape, self.on, self.take = shape, on, take


def rows_units(g, kd, width, x, tiles, c0, cw, take, on=("act", "dve")):
    out = []
    for t in tiles:
        for c in range(c0, c0 + cw, 512):
            wd = min(512, c0 + cw - c)
            out.append(Unit(g, kd, width, lambda w, k, t=t: x[:, k, t * P:(t + 1) * P],
                            lambda w, k, c=c, wd=wd: w[:, k, c:c + wd], (P, wd), on[len(out) % len(on)],
                            lambda e, bank, inc, t=t, c=c, wd=wd: take(e, bank, inc, t, c - c0, wd)))
    return out


def cols_units(g, kd, width, x, spans, chunks, pick, take, on=("act", "dve")):
    out = []
    for c in chunks:
        for a, n in spans:
            out.append(Unit(g, kd, width, lambda w, k, c=c: pick(w, k, c), lambda w, k, a=a, n=n: x[:, k, a:a + n],
                            (P, n), on[len(out) % len(on)], lambda e, bank, inc, c=c, a=a, n=n: take(e, bank, inc, c, a, n)))
    return out


def stage_products(K, name, ngroups, units):
    ps = K.ps
    n0 = K.w.used
    to_act = [i for i, u in enumerate(units) if u.on == "act"]
    to_dve = [i for i, u in enumerate(units) if u.on != "act"]
    E, S, V = K.steps("product", pe=[f"u{i}" for i in range(len(units))], act=[f"e{i}" for i in to_act],
                      dve=[f"e{i}" for i in to_dve])
    for i, u in enumerate(units):
        K.w.free[n0 + u.g] = E.at(f"u{i}")
    K.w.used = n0 + ngroups
    with K.nc.Block() as block:
        @block.sync
        def _(sp):
            K.w.issue(sp, K.w.used + K.w.ring)

        @block.tensor
        def _(pe):
            seen = -1
            for i, u in enumerate(units):
                w = K.w.slot(n0 + u.g, u.kd, u.width)
                if u.g != seen:
                    pe.wait_ge(*K.w.landed_at(n0 + u.g))
                    seen = u.g
                if i >= 8:
                    pe.wait_ge(*(S if units[i - 8].on == "act" else V).at(f"e{i - 8}"))
                for k in range(u.kd):
                    mm = pe.matmul(ps[i % 8][0:u.shape[0], 0:u.shape[1]], u.lhs(w, k), u.rhs(w, k), start=k == 0,
                                   stop=k == u.kd - 1)
                mm.then_inc(*E(f"u{i}"))

        @block.scalar
        def _(act):
            for i in to_act:
                act.wait_ge(*E.at(f"u{i}"))
                units[i].take(act, ps[i % 8][0:units[i].shape[0], 0:units[i].shape[1]], S(f"e{i}"))

        @block.vector
        def _(dve):
            for i in to_dve:
                dve.wait_ge(*E.at(f"u{i}"))
                units[i].take(dve, ps[i % 8][0:units[i].shape[0], 0:units[i].shape[1]], V(f"e{i}"))


def copy_to(K, e, dst, bank, inc):
    if e is K.nc.scalar:
        e.activation(dst, bank, ACT.Copy).then_inc(*inc)
    else:
        e.tensor_copy(dst, bank).then_inc(*inc)


def func_to(func):
    return lambda e, dst, bank, inc: e.activation(dst, bank, func).then_inc(*inc)


class Second:

    def __init__(self, K, mem):
        nc = K.nc
        q = K.ring[:, 3:6, :].rearrange("p a n -> p (a n)")
        self.quarter = [q[:, 3072 * i:3072 * (i + 1)] for i in range(4)]
        self.lower, self.upper = q[:, 0:6144], q[:, 6144:12288]
        self.C = mem.enter_context(nc.sbuf_tensor("ctx_rows", [P, 2, D], F32))
        self.CT = mem.enter_context(nc.sbuf_tensor("ctx_cols", [P, KD, CTX], F32))
        self.KB = mem.enter_context(nc.sbuf_tensor("shared_keys", [P, 1, TA], F32))
        self.VB = mem.enter_context(nc.sbuf_tensor("shared_vals", [P, 6, P], F32))
        self.cc = mem.enter_context(nc.sbuf_tensor("cond", [P, KD, 2], F32))
        self.ba = mem.enter_context(nc.sbuf_tensor("b_ada", [P, DEPTH, 24], F32))
        self.ng = mem.enter_context(nc.sbuf_tensor("norm_g", [P, DEPTH, KD], F32))
        self.hg = mem.enter_context(nc.sbuf_tensor("head_g", [P, DEPTH, 4], F32))
        self.mod = mem.enter_context(nc.sbuf_tensor("mod", [P, 24, 2], F32))
        self.sc = mem.enter_context(nc.sbuf_tensor("mod_scale", [P, 2, KD], F32))
        self.sh = mem.enter_context(nc.sbuf_tensor("mod_shift", [P, 2, KD], F32))
        self.rpb = [nc.dram_tensor(f"rpb_wide_{l}", [HEADS * RPB_R, 127], F32, kind="Internal").ap() for l in range(DEPTH)]

        self.bias = [nc.dram_tensor(f"rpb_bias_{l}", [HEADS, 64, RPB_R, 64], F32, kind="Internal").ap() for l in range(DEPTH)]


def rows_of(x, w):
    return x.rearrange("p (t n) -> p t n", n=w)


def stage_second_start(K, B):
    nc, A = K.nc, K.A
    with nc.sbuf_tensor("rpb_wide", [HEADS * RPB_R, DEPTH, 127], F32) as wide:
        V, S = K.steps("second_start", dve=["zero", "gq0", "gq1"], act=["c"])
        into = nc.alloc_semaphore("rpb_landed")
        outof = nc.alloc_semaphore("rpb_stored")
        with nc.Block() as block:
            @block.sync
            def _(sp):
                K.load(sp, B.C[:, :, :], A["ctx_2"][0].rearrange("(t p) d -> p t d", p=P))
                with nc.allow_non_contiguous_dma(reason="parameters as columns, once"):
                    K.load(sp, B.cc[:, :, 0], A["c_2"][0].rearrange("(k p) -> p k", p=P))
                    K.load(sp, B.cc[:, :, 1], A["c_ctx_2"].rearrange("(k p) -> p k", p=P))
                    for l in range(DEPTH):
                        K.load(sp, B.ba[:, l, :], A["b_ada_2"][l].rearrange("(c p) -> p c", p=P))
                        K.load(sp, B.ng[:, l, :], A["norm_g_2"][l].rearrange("(c p) -> p c", p=P))
                        for i, n in enumerate(("q_norm_a_2", "k_norm_a_2", "q_norm_b_2", "k_norm_b_2")):
                            for half in range(2):
                                K.load(sp, B.hg[64 * half:64 * half + 64, l, i:i + 1], A[n][l:l + 1].rearrange("a n -> n a"))
                K.w.issue(sp, K.w.used + K.w.ring)

            @block.gpsimd
            def _(pool):
                pool.wait_ge(*V.at("zero"))
                for l in range(DEPTH):
                    pool.dma_start(wide[:, l, 48:48 + RPB_C], A["rpb_2"][l].rearrange("h r c -> (h r) c")).then_inc(into, 16)
                pool.wait_ge(into, 32)
                for l in range(DEPTH):
                    pool.dma_start(B.rpb[l], wide[:, l, :]).then_inc(outof, 16)
                pool.wait_ge(outof, 32)
                for l in range(DEPTH):
                    for h in range(HEADS):
                        src = bass.AP(B.rpb[l].tensor, h * RPB_R * 127 + 63, [[127, RPB_R], [-1, 64], [1, 64]])
                        pool.dma_start(B.bias[l][h].rearrange("q i n -> i q n"), src).then_inc(outof, 16)
                pool.wait_ge(outof, 32 + 16 * DEPTH * HEADS)

            @block.scalar
            def _(act):
                act.wait_ge(K.loaded, K.n_loaded)
                act.activation(B.cc[:, :, :], B.cc[:, :, :], ACT.Silu).then_inc(*S("c"))

            @block.vector
            def _(dve):
                dve.memset(wide[:, :, :], 0.0).then_inc(*V("zero"))
                dve.wait_ge(K.loaded, K.n_loaded)
                for i in (0, 2):
                    dve.tensor_scalar(B.hg[:, :, i], B.hg[:, :, i], 0.125, None, ALU.mult).then_inc(*V(f"gq{i // 2}"))


def stage_mod(K, B, l):
    units = []
    for g in range(6):
        def take(e, bank, inc, c, a, n, g=g):
            ch = 4 * g + c
            if e is K.nc.scalar:
                e.activation(B.mod[:, ch, :], bank, ACT.Identity, bias=B.ba[:, l, ch:ch + 1]).then_inc(*inc)
            else:
                e.tensor_scalar(B.mod[:, ch, :], bank, B.ba[:, l, ch:ch + 1], None, ALU.add).then_inc(*inc)
        units += cols_units(g, KD, 512, B.cc, [(0, 2)], range(4), lambda w, k, c: w[:, k, c * P:(c + 1) * P], take)
    stage_products(K, f"mod{l}", 6, units)


def stage_row_norm(K, B, l, Xn, Cn):
    nc = K.nc
    tiles = [(K.H, Xn, t) for t in range(NT)] + [(B.C, Cn, t) for t in range(2)]
    n = range(len(tiles))
    with ExitStack() as mem:
        ss = mem.enter_context(nc.sbuf_tensor(f"rn_ss{l}", [P, len(tiles)], F32))
        S, V = K.steps("row_norm", act=[f"q{i}" for i in n] + ["ln", "rs"] + [f"n{i}" for i in n if i % 2 == 0],
                       dve=["s0", "s1", "g0", "g1", "h0", "h1"] + [f"n{i}" for i in n if i % 2])
        with nc.Block() as block:
            @block.sync
            def _(sp):
                K.w.issue(sp, K.w.used + K.w.ring)

            @block.scalar
            def _(act):
                for i, (x, y, t) in enumerate(tiles):
                    act.activation(y[:, t, :], x[:, t, :], ACT.Square, accum_out=ss[:, i:i + 1]).then_inc(*S(f"q{i}"))
                act.wait_ge(*S.at(f"q{len(tiles) - 1}"))
                act.activation(ss[:, :], ss[:, :], ACT.Ln, scale=1.0 / D, bias=K.c("eps")[:, 0:1]).then_inc(*S("ln"))
                act.wait_ge(*S.at("ln"))
                act.activation(ss[:, :], ss[:, :], ACT.Exp, scale=-0.5).then_inc(*S("rs"))
                act.wait_ge(*S.at("rs"))
                for i, (x, y, t) in enumerate(tiles):
                    if i % 2 == 0:
                        act.activation(y[:, t, :], x[:, t, :], ACT.Copy, scale=ss[:, i:i + 1]).then_inc(*S(f"n{i}"))

            @block.vector
            def _(dve):
                for j in range(2):
                    dve.tensor_scalar(B.sc[:, j, :], B.mod[:, 8:16, j], 1.0, None, ALU.add).then_inc(*V(f"s{j}"))
                for j in range(2):
                    dve.wait_ge(*V.at("s1"))
                    dve.tensor_tensor(B.sc[:, j, :], B.sc[:, j, :], B.ng[:, l, :], ALU.mult).then_inc(*V(f"g{j}"))
                for j in range(2):
                    dve.tensor_copy(B.sh[:, j, :], B.mod[:, 0:8, j]).then_inc(*V(f"h{j}"))
                dve.wait_ge(*S.at("rs"))
                for i, (x, y, t) in enumerate(tiles):
                    if i % 2:
                        dve.tensor_scalar(y[:, t, :], x[:, t, :], ss[:, i:i + 1], None, ALU.mult).then_inc(*V(f"n{i}"))


def stage_head_norm(K, name, pieces, rope):
    nc, ps = K.nc, K.ps
    n = len(pieces)
    r = range(n)
    turned = [i for i in r if pieces[i][2] is not None]

    def after(i):
        return [i - 1] if i - 1 in turned else []
    with ExitStack() as mem:
        sq = mem.enter_context(nc.sbuf_tensor(f"{name}_sq", [P, 2, 512], F32))
        tmp = mem.enter_context(nc.sbuf_tensor(f"{name}_tmp", [P, 2, 512], F32))
        tab = mem.enter_context(nc.sbuf_tensor(f"{name}_tab", [P, 2, T], F32))
        act_l, dve_l, pe_l = ["q0"], [], []
        for i in r:
            act_l += ([f"q{i + 1}"] if i + 1 < n else []) + [f"l{i}", f"r{i}"]
        for i in range(n + 1):
            dve_l += ([f"n{i}"] if i < n else []) + [f"{x}{j}" for j in after(i) for x in ("s", "c", "a")]
            pe_l += ([f"m{i}"] if i < n else []) + [f"p{j}" for j in after(i)]
        E, S, V = K.steps("head_norm", pe=pe_l, act=act_l, dve=dve_l)

        def w(i):
            return pieces[i][0].shape[1]

        with nc.Block() as block:
            @block.sync
            def _(sp):
                K.load(sp, tab[:, :, :], K.A["rope"].rearrange("p (a n) -> p a n", a=2))
                K.w.issue(sp, K.w.used + K.w.ring)

            @block.tensor
            def _(pe):
                for i in range(n + 1):
                    if i < n:
                        pe.wait_ge(*S.at(f"q{i}"))
                        if i >= 4:
                            pe.wait_ge(*S.at(f"l{i - 4}"))
                        pe.matmul(ps[i % 4][:, 0:w(i)], K.c("half_ones"), sq[:, i % 2, 0:w(i)], start=True,
                                  stop=True).then_inc(*E(f"m{i}"))
                    for j in after(i):
                        pe.wait_ge(*V.at(f"n{j}"))
                        if [x for x in turned if x <= j - 4]:
                            pe.wait_ge(*V.at(f"s{max(x for x in turned if x <= j - 4)}"))
                        pe.matmul(ps[4 + j % 4][:, 0:w(j)], K.c("swap"), pieces[j][0], start=True, stop=True).then_inc(*E(f"p{j}"))

            @block.scalar
            def _(act):
                def square(i):
                    if i >= 2:
                        act.wait_ge(*V.at(f"n{i - 2}"))
                    act.activation(sq[:, i % 2, 0:w(i)], pieces[i][0], ACT.Square).then_inc(*S(f"q{i}"))
                square(0)
                for i in r:
                    if i + 1 < n:
                        square(i + 1)
                    act.wait_ge(*E.at(f"m{i}"))
                    act.activation(sq[:, i % 2, 0:w(i)], ps[i % 4][:, 0:w(i)], ACT.Ln, scale=1.0 / 64,
                                   bias=K.c("eps")[:, 0:1]).then_inc(*S(f"l{i}"))
                    act.wait_ge(*S.at(f"l{i}"))
                    act.activation(sq[:, i % 2, 0:w(i)], sq[:, i % 2, 0:w(i)], ACT.Exp, scale=-0.5).then_inc(*S(f"r{i}"))

            @block.vector
            def _(dve):
                dve.wait_ge(K.loaded, K.n_loaded)
                for i in range(n + 1):
                    if i < n:
                        x, g, _ = pieces[i]
                        dve.wait_ge(*S.at(f"r{i}"))
                        dve.scalar_tensor_tensor(x, x, g, sq[:, i % 2, 0:w(i)], ALU.mult, ALU.mult).then_inc(*V(f"n{i}"))
                    for j in after(i):
                        x, _, (a, m) = pieces[j]
                        dve.wait_ge(*E.at(f"p{j}"))
                        dve.tensor_tensor(tmp[:, j % 2, 0:m], ps[4 + j % 4][:, 0:m], tab[:, 1, a:a + m], ALU.mult).then_inc(*V(f"s{j}"))
                        dve.tensor_tensor(x, x, tab[:, 0, a:a + m], ALU.mult).then_inc(*V(f"c{j}"))
                        dve.wait_ge(*V.at(f"c{j}"))
                        dve.tensor_tensor(x, x, tmp[:, j % 2, 0:m], ALU.add).then_inc(*V(f"a{j}"))


def stage_multiply(K, name, pairs, op=ALU.mult):
    V, = K.steps("multiply", dve=[f"m{i}" for i in range(len(pairs))])
    with K.nc.Block() as block:
        @block.sync
        def _(sp):
            K.w.issue(sp, K.w.used + K.w.ring)

        @block.vector
        def _(dve):
            for i, (x, y) in enumerate(pairs):
                dve.tensor_tensor(x, x, y, op).then_inc(*V(f"m{i}"))


def stage_gate_rows(K, B, l, GB, right):
    nc, ps = K.nc, K.ps
    E, S, V = K.steps("gate_rows", pe=["g0", "g1"], act=["c0", "c1"], dve=["r0", "r1"])
    with nc.Block() as block:
        @block.sync
        def _(sp):
            K.w.issue(sp, K.w.used + K.w.ring)

        @block.vector
        def _(dve):
            for j in range(2):
                dve.tensor_tensor(right[:, j, :].rearrange("p (k n) -> p k n", k=KD), bm(K.c("ident"), KD),
                                  bc(B.mod[:, 16:24, j], P), ALU.mult).then_inc(*V(f"r{j}"))

        @block.tensor
        def _(pe):
            for j in range(2):
                pe.wait_ge(*V.at(f"r{j}"))
                for c in range(2):
                    mm = pe.matmul(ps[2 * j + c], K.c("ones"), right[:, j, c * 512:c * 512 + 512], start=True, stop=True)
                mm.then_inc(*E(f"g{j}"))

        @block.scalar
        def _(act):
            for j in range(2):
                act.wait_ge(*E.at(f"g{j}"))
                act.activation(GB[:, j, :], K.bank[:, 2 * j:2 * j + 2, :].rearrange("p a n -> p (a n)"), ACT.Copy).then_inc(*S(f"c{j}"))


def plan_second(K, l):
    w = K.A["w_in_2"][l]
    for g in range(6):
        plan_gemm(K, K.A["w_ada_2"][l], 512 * g, 512, KD)
    for c0, n in ((0, 512), (512, 512), (1024, 256), (1280, 512), (1792, 512), (2304, 512), (2816, 512),
                  (3328, 512), (3840, 512)):
        if c0 == 1792:
            cols = [c0 + 256 * a + 64 * c for c in range(4) for a in range(2)]
            K.w.loads.append(([w.rearrange("(k p) n -> p k n", p=P)[:, :, a:a + 64] for a in cols], KD, n))
        else:
            plan_gemm(K, w, c0, n, KD)
    plan_gemm(K, K.A["w_o_a_2"][l], 0, D, 4)
    for c0 in (4352, 4864):
        plan_gemm(K, w, c0, 512, KD)
    plan_gemm(K, K.A["w_o_b_2"][l], 0, D, 4)
    for g in range(2):
        plan_gemm(K, K.A["w_out_2"][l], 512 * g, 512, KD)


def second_layer(K, B, l):
    nc = K.nc
    with_ctx = l < DEPTH - 1
    stage_mod(K, B, l)
    Xn = K.OT[:, :, :].rearrange("p (t a) n -> p t (a n)", t=NT)
    with nc.sbuf_tensor(f"ctx_normed{l}", [P, 2, D], F32) as Cn:
        stage_row_norm(K, B, l, Xn, Cn)
        stage_to_cols(K, f"mixer_cols{l}", Xn, K.HT, NT, scale=B.sc[:, 0, :], shift=B.sh[:, 0, :])
        stage_to_cols(K, f"mixer_ctx_cols{l}", Cn, B.CT, 2, scale=B.sc[:, 1, :], shift=B.sh[:, 1, :])
    q3 = [x.rearrange("p (c n) -> p c n", n=TA) for x in B.quarter]
    r3 = [x.rearrange("p (t n) -> p t n", n=NA_W) for x in B.quarter]
    QA, VA, KA, QB = q3[0], r3[1], q3[2], q3[3]

    def plain(w, k, c):
        return w[:, k, c * P:(c + 1) * P]

    def cols_to(dst, off):
        return lambda e, bank, inc, c, a, n: copy_to(K, e, dst[:, c, off + a:off + a + n], bank, inc)

    def rows_to(dst, t0):
        return lambda e, bank, inc, t, c, n: copy_to(K, e, dst[:, t0 + t, c:c + n], bank, inc)

    def both_cols(g, width, chunks, pick, dst, ctx=True):
        return (cols_units(g, KD, width, K.HT, [(0, T)], chunks, pick, cols_to(dst, 0)) +
                (cols_units(g, KD, width, B.CT, [(0, CTX)], chunks, pick, cols_to(dst, T)) if ctx else []))

    def both_rows(g, kd, width, xT, cT, c0, cw, take, ctx=True, on=("act", "dve")):
        return (rows_units(g, kd, width, xT, range(NT), c0, cw, take(0), on) +
                (rows_units(g, kd, width, cT, range(2), c0, cw, take(NT), on) if ctx else []))

    units = both_cols(0, 512, range(4), plain, KA)
    units += both_rows(1, KD, 512, K.HT, B.CT, 0, 512, lambda t0: rows_to(VA, t0))
    units += both_cols(2, 256, range(1), plain, B.KB)
    units += both_rows(2, KD, 256, K.HT, B.CT, P, P, lambda t0: rows_to(B.VB, t0))
    units += both_cols(3, 512, range(4), plain, QA, with_ctx)
    units += both_cols(4, 512, range(4), plain, QB, with_ctx)
    stage_products(K, f"qkv{l}", 5, units)

    def g(i):
        return B.hg[:, l, i:i + 1]
    ctx = slice(T, TA)
    pieces = [(KA[:, c, s], g(1), None) for c in range(4) for s in (slice(0, T), ctx)]
    pieces += [(QA[:, c, s], g(0), None) for c in range(4) for s in (slice(0, T), ctx)[:1 + with_ctx]]
    pieces += [(B.KB[:, 0, 0:T], g(3), (0, T)), (B.KB[:, 0, ctx], g(3), None)]
    pieces += [(QB[:, c, 0:T], g(2), (0, T)) for c in range(4)]
    pieces += [(QB[:, c, ctx], g(2), None) for c in range(4) if with_ctx]
    stage_head_norm(K, f"head_norm{l}", pieces, None)

    OA = K.OT[:, :, :].rearrange("p a n -> p (a n)")[:, 0:6 * NA_W].rearrange("p (t n) -> p t n", n=NA_W)
    stage_attention(K, f"window{l}", "pairs", QA, KA, VA, OA, 4, NT, TA, rpb=B.bias[l])
    if with_ctx:
        stage_attention(K, f"window_ctx{l}", "pairs", QA[:, :, ctx], KA[:, :, ctx], VA[:, NT:, :], OA[:, NT:, :], 4, 2, CTX)
    OB = r3[0]
    stage_attention(K, f"shared{l}", "shared", QB, B.KB, B.VB, OB, 4, NT, TA)
    if with_ctx:
        stage_attention(K, f"shared_ctx{l}", "shared", QB[:, :, ctx], B.KB[:, :, ctx], B.VB[:, NT:, :], OB[:, NT:, :], 4, 2, CTX)

    ZA, ZB = r3[2], r3[1]

    def act_rows(func, dst):
        return lambda t0: lambda e, bank, inc, t, c, n: func_to(func)(e, dst[:, t0 + t, c:c + n], bank, inc)
    units = both_rows(0, KD, 512, K.HT, B.CT, 0, 512, act_rows(ACT.Silu, ZA), with_ctx, ("act",))
    units += both_rows(1, KD, 512, K.HT, B.CT, 0, 512, act_rows(ACT.Silu, ZB), with_ctx, ("act",))
    stage_products(K, f"z{l}", 2, units)
    nt = NT + 2 * with_ctx
    stage_multiply(K, f"times_z{l}", [(x[:, t, :], z[:, t, :]) for x, z in ((OA, ZA), (OB, ZB)) for t in range(nt)])
    CA, CB = q3[3], q3[2]
    for n, src, dst in ((f"oa_cols{l}", OA, CA), (f"ob_cols{l}", OB, CB)):
        stage_to_cols(K, n, src, dst, NT, kd=4)
        if with_ctx:
            stage_to_cols(K, n + "_ctx", src[:, NT:, :], dst[:, :, ctx], 2, kd=4)

    with ExitStack() as mem:
        M1 = rows_of(B.lower, D)
        M2 = mem.enter_context(nc.sbuf_tensor(f"merged{l}", [P, 6, D], F32))
        for i, (M, cols) in enumerate(((M1, CA), (M2, CB))):
            def sig(off):
                return lambda t0: lambda e, bank, inc, t, c, n: func_to(ACT.Sigmoid)(e, M[:, t0 + t, off + c:off + c + n], bank, inc)

            def times(t0):
                def take(e, bank, inc, t, c, n):
                    d = M[:, t0 + t, c:c + n]
                    e.tensor_tensor(d, d, bank, ALU.mult).then_inc(*inc)
                return take
            units = both_rows(0, KD, 512, K.HT, B.CT, 0, 512, sig(0), with_ctx, ("act",))
            units += both_rows(1, KD, 512, K.HT, B.CT, 0, 512, sig(512), with_ctx, ("act",))
            stage_products(K, f"gate{i}_{l}", 2, units)
            stage_products(K, f"o{i}_{l}", 1, both_rows(0, 4, D, cols[:, :, 0:T], cols[:, :, ctx], 0, D, times, with_ctx, ("dve",)))
        stage_multiply(K, f"merge{l}", [(M1[:, t, :], M2[:, t, :]) for t in range(nt)], ALU.add)
    MC = B.upper.rearrange("p (c n) -> p c n", n=TA)
    stage_to_cols(K, f"merged_cols{l}", M1, MC, NT)
    if with_ctx:
        stage_to_cols(K, f"merged_ctx_cols{l}", M1[:, NT:, :], MC[:, :, ctx], 2)
    with nc.sbuf_tensor(f"gate_b{l}", [P, 2, D], F32) as GB:
        right = B.lower[:, 0:2 * D].rearrange("p (a n) -> p a n", a=2)
        tmp = B.lower[:, 0:2048].rearrange("p (a n) -> p a n", a=4)
        stage_gate_rows(K, B, l, GB, right)
        units = []
        for gp in range(2):
            def take(t0, gp=gp):
                def f(e, bank, inc, t, c, n):
                    j = 0 if t0 == 0 else 1
                    d = (K.H if j == 0 else B.C)[:, t, 512 * gp:512 * gp + 512]
                    m = tmp[:, t % 4, :]
                    e.tensor_tensor(m, bank, GB[:, j, 512 * gp:512 * gp + 512], ALU.mult).then_inc(K.gated, 1)
                    K.n_gated += 1
                    e.wait_ge(K.gated, K.n_gated)
                    e.tensor_tensor(d, d, m, ALU.add).then_inc(*inc)
                return f
            units += both_rows(gp, KD, 512, MC[:, :, 0:T], MC[:, :, ctx], 0, 512, take, with_ctx, ("dve",))
        stage_products(K, f"mixer_out{l}", 2, units)


def start_second_ring(K):
    K.w = Weights(K.nc, "weights2", K.ring[:, 0:RING2, :], RING2)
    K.gated = K.nc.alloc_semaphore("gated_result")
    K.n_gated = 0
    for l in range(DEPTH):
        plan_second(K, l)


def second_block(K):
    with ExitStack() as mem:
        B = Second(K, mem)
        stage_second_start(K, B)
        for l in range(DEPTH):
            second_layer(K, B, l)


def stage_store(K):
    stored = K.nc.alloc_semaphore("out_stored")
    with K.nc.Block() as block:
        @block.sync
        def _(sp):
            sp.dma_start(K.out.rearrange("(t p) d -> p t d", p=P), K.H[:, :, :]).then_inc(stored, 16)
            sp.wait_ge(stored, 16)


def build(nc, A, out):
    K = Kernel(nc, A, out)
    X = Experts(K)
    plan_dn_projection(K)
    for g in range(2):
        plan_gemm(K, A["a_w_out"][0], 512 * g, 512, KD)
    plan_experts(K, 0)
    plan_differential(K)
    plan_experts(K, 1)
    stage_start(K)
    stage_clear_block_rows(K, X)
    delta_net(K)
    stage_layer_norm(K, "ln_mix0", K.H, A["ln_mix_g"][0], A["ln_mix_b"][0])
    moe_layer(K, X, 0)
    differential(K)
    stage_layer_norm(K, "ln_mix1", K.H, A["ln_mix_g"][1], A["ln_mix_b"][1])
    moe_layer(K, X, 1)
    start_second_ring(K)
    second_block(K)
    stage_store(K)


_INS = ["x", "a_w_in", "a_conv_w", "a_a_log", "a_dt_bias", "a_norm_w", "a_w_out", "kv_w", "b_w_q", "b_lambda",
        "b_subln_w", "b_w_out", "ln_mix_g", "ln_mix_b", "ln_ffn_g", "ln_ffn_b", "moe_w_group", "moe_w_expert",
        "moe_w13", "moe_w2", "c_2", "ctx_2", "c_ctx_2", "w_ada_2", "b_ada_2", "norm_g_2", "w_in_2", "q_norm_a_2",
        "k_norm_a_2", "q_norm_b_2", "k_norm_b_2", "rpb_2", "w_o_a_2", "w_o_b_2", "w_out_2"]


def kernel(**inputs):
    import concourse.bacc as bacc
    from concourse.bass_utils import run_bass_kernel_spmd

    nc = bacc.Bacc("TRN2", target_bir_lowering=False, num_devices=1)
    arrays = {name: np.ascontiguousarray(inputs[name]) for name in _INS}
    arrays["consts"] = CONST_ARRAY
    arrays["rope"] = rope_tables()
    A = {name: nc.dram_tensor(f"in_{name}", a.shape, mybir.dt.from_np(a.dtype), kind="ExternalInput").ap()
         for name, a in arrays.items()}
    out = nc.dram_tensor("out_0", (T, D), F32, kind="ExternalOutput").ap()
    build(nc, A, out)
    r = run_bass_kernel_spmd(nc, [{f"in_{name}": a for name, a in arrays.items()}], core_ids=[0])
    return r.results[0]["out_0"].reshape(1, T, D)
```
